# Optimizing a Trainium2 kernel written in Bass

```python
import math
import jax
import jax.numpy as jnp
from jax import lax
import numpy as np

D_MODEL = 1024
BATCH = 1
SEQ = 256
DEPTH = 1

GRID_W = 64
CTX_LEN = 256

HEAD_DIM = 64
N_Q_HEADS = 8
N_KV_HEADS = 2
D_Q = N_Q_HEADS * HEAD_DIM
D_KV = N_KV_HEADS * HEAD_DIM
WINDOW = 128
ATTN_BLOCK = 128
ROPE_BASE = 10000.0

D_SSM = D_MODEL // 4
SSM_GROUP = 16
N_SSM_GROUPS = D_SSM // SSM_GROUP
SSM_STATE = 64

D_CONV = D_MODEL // 4
CONV_WIDTH = 3

N_BRANCH = 3
IN_SIZES = (D_SSM, D_CONV, D_CONV, D_CONV, D_Q, D_KV, D_KV, N_BRANCH * D_MODEL)
D_IN = sum(IN_SIZES)

N_EXPERTS = 32
TOP_K = 4
D_EXPERT = D_MODEL
SWIGLU_LIMIT = 7.0
SWIGLU_ALPHA = 1.702
MOE_BLOCK = 256

EPS = 1e-6

kernel_name = 'hybrid_s5_conv_swa_moe_dit'

def rms_norm(x, g):
    xf = x.astype(jnp.float32)
    y = xf * lax.rsqrt(jnp.mean(xf * xf, axis=-1, keepdims=True) + EPS)
    return (y * g.astype(jnp.float32)).astype(x.dtype)

def modulate(h, shift, scale):
    return h * (1.0 + scale) + shift

def softmax_with_sink(logits, sink):
    sink_col = jnp.broadcast_to(sink, logits.shape[:-1] + (1,))
    probs = jax.nn.softmax(jnp.concatenate([logits, sink_col], axis=-1), axis=-1)
    return probs[..., :-1]

def axial_rope(n_lat):
    rows = n_lat // GRID_W
    t = jnp.arange(rows * GRID_W)
    row = (t // GRID_W).astype(jnp.float32)
    col = (t % GRID_W).astype(jnp.float32)
    n_pairs = HEAD_DIM // 4
    inv_freq = ROPE_BASE ** (-jnp.arange(n_pairs, dtype=jnp.float32) / n_pairs)
    ang = jnp.concatenate([row[:, None] * inv_freq, col[:, None] * inv_freq], axis=-1)
    return jnp.cos(ang), jnp.sin(ang)

def apply_rope(x, cos, sin):
    xf = x.astype(jnp.float32)
    x1, x2 = jnp.split(xf, 2, axis=-1)
    c = cos[None, :, None, :]
    s = sin[None, :, None, :]
    return jnp.concatenate([x1 * c - x2 * s, x1 * s + x2 * c], axis=-1).astype(x.dtype)

def _linear_recurrence(left, right):
    a_l, b_l = left
    a_r, b_r = right
    return a_l * a_r, a_r * b_l + b_r

def s5_bidirectional(u_c, u_l, lam_re, lam_im, log_dt, b_re, b_im, c_re, c_im, d_skip):
    f32 = jnp.float32
    bsz, n_ctx, _ = u_c.shape
    n_lat = u_l.shape[1]
    n_tot = n_ctx + n_lat
    lam = lax.complex(lam_re.astype(f32), lam_im.astype(f32))
    dt = jnp.exp(log_dt.astype(f32))[..., None]
    lam_bar = jnp.exp(lam * dt)
    b_bar = ((lam_bar - 1.0) / lam)[..., None] * lax.complex(b_re.astype(f32), b_im.astype(f32))
    c_mat = lax.complex(c_re.astype(f32), c_im.astype(f32))
    seq_fwd = jnp.concatenate([u_c, u_l], axis=1)
    seq_bwd = jnp.concatenate([u_c[:, ::-1], u_l[:, ::-1]], axis=1)
    u = jnp.stack([seq_fwd, seq_bwd]).astype(f32).reshape(2, bsz, n_tot, N_SSM_GROUPS, SSM_GROUP)
    bu = jnp.einsum('zbtgh,zgph->zbtgp', u.astype(jnp.complex64), b_bar)
    a = jnp.broadcast_to(lam_bar[:, None, None], (2, 1, n_tot, N_SSM_GROUPS, SSM_STATE))
    _, states = lax.associative_scan(_linear_recurrence, (a, bu), axis=2)
    y = jnp.einsum('zbtgp,zghp->zbtgh', states, c_mat).real.reshape(2, bsz, n_tot, D_SSM)
    y_c = y[0, :, :n_ctx] + y[1, :, :n_ctx][:, ::-1]
    y_l = y[0, :, n_ctx:] + y[1, :, n_ctx:][:, ::-1]
    d = d_skip.astype(f32)
    out_c = (y_c + d * u_c.astype(f32)).astype(u_c.dtype)
    out_l = (y_l + d * u_l.astype(f32)).astype(u_l.dtype)
    return out_c, out_l

def short_conv_mixer(b_gate, c_gate, x_in, conv_w):
    z = c_gate * x_in
    taps = conv_w[:, None, :].astype(z.dtype)
    pad = CONV_WIDTH // 2
    zc = lax.conv_general_dilated(z, taps, window_strides=(1,), padding=[(pad, pad)],
                                  dimension_numbers=('NWC', 'WIO', 'NWC'),
                                  feature_group_count=D_CONV)
    return b_gate * zc

def context_attention(q_c, k_c, v_c, sinks):
    bsz, n_ctx = q_c.shape[:2]
    rep = N_Q_HEADS // N_KV_HEADS
    q = q_c.reshape(bsz, n_ctx, N_KV_HEADS, rep, HEAD_DIM)
    s = jnp.einsum('blgrd,bmgd->bgrlm', q, k_c).astype(jnp.float32) * HEAD_DIM ** -0.5
    p = softmax_with_sink(s, sinks.astype(jnp.float32).reshape(1, N_KV_HEADS, rep, 1, 1))
    o = jnp.einsum('bgrlm,bmgd->blgrd', p.astype(v_c.dtype), v_c)
    return o.reshape(bsz, n_ctx, D_Q)

def windowed_latent_attention(q_l, k_l, v_l, k_c, v_c, sinks):
    bsz, n_lat = q_l.shape[:2]
    rep = N_Q_HEADS // N_KV_HEADS
    blk = ATTN_BLOCK
    nb = n_lat // blk
    scale = HEAD_DIM ** -0.5
    sink = sinks.astype(jnp.float32).reshape(1, N_KV_HEADS, rep, 1, 1)

    def band(t):
        tp = jnp.pad(t, ((0, 0), (blk, blk), (0, 0), (0, 0))).reshape(bsz, nb + 2, blk, N_KV_HEADS, HEAD_DIM)
        tb = jnp.concatenate([tp[:, :-2], tp[:, 1:-1], tp[:, 2:]], axis=2)
        return jnp.moveaxis(tb, 1, 0)

    q_blocks = jnp.moveaxis(q_l.reshape(bsz, nb, blk, N_KV_HEADS, rep, HEAD_DIM), 1, 0)
    k_band = band(k_l)
    v_band = band(v_l)
    q_pos = jnp.arange(nb)[:, None] * blk + jnp.arange(blk)[None, :]
    k_pos = (jnp.arange(nb)[:, None] - 1) * blk + jnp.arange(3 * blk)[None, :]
    valid = ((jnp.abs(q_pos[:, :, None] - k_pos[:, None, :]) <= WINDOW)
             & (k_pos[:, None, :] >= 0) & (k_pos[:, None, :] < n_lat))

    def one_block(args):
        q, k, v, m = args
        s_loc = jnp.einsum('bqgrd,bkgd->bgrqk', q, k).astype(jnp.float32) * scale
        s_loc = jnp.where(m, s_loc, -jnp.inf)
        s_ctx = jnp.einsum('bqgrd,bmgd->bgrqm', q, k_c).astype(jnp.float32) * scale
        p = softmax_with_sink(jnp.concatenate([s_loc, s_ctx], axis=-1), sink).astype(v.dtype)
        return (jnp.einsum('bgrqk,bkgd->bqgrd', p[..., :3 * blk], v)
                + jnp.einsum('bgrqm,bmgd->bqgrd', p[..., 3 * blk:], v_c))

    o = lax.map(one_block, (q_blocks, k_band, v_band, valid))
    return jnp.moveaxis(o, 0, 1).reshape(bsz, n_lat, D_Q)

def branch_merge(y_ssm, y_conv, y_attn, gate_logits, p):
    z = jax.nn.gelu(y_ssm)
    br_ssm = (z * jax.nn.sigmoid(z @ p['w_glu'])) @ p['w_ssm_out']
    br_conv = y_conv @ p['w_conv_out']
    br_attn = y_attn @ p['w_attn_out']
    g_ssm, g_conv, g_attn = jnp.split(jax.nn.sigmoid(gate_logits), N_BRANCH, axis=-1)
    return (g_ssm * br_ssm + g_conv * br_conv + g_attn * br_attn) @ p['w_o']

def hybrid_mixer(h_c, h_l, p, with_ctx_out):
    splits = np.cumsum(IN_SIZES)[:-1].tolist()
    u_c, cb_c, cc_c, cx_c, q_c, k_c, v_c, gt_c = jnp.split(h_c @ p['w_in'], splits, axis=-1)
    u_l, cb_l, cc_l, cx_l, q_l, k_l, v_l, gt_l = jnp.split(h_l @ p['w_in'], splits, axis=-1)
    n_lat = h_l.shape[1]

    ys_c, ys_l = s5_bidirectional(u_c, u_l, p['ssm_lam_re'], p['ssm_lam_im'], p['ssm_log_dt'],
                                  p['ssm_b_re'], p['ssm_b_im'], p['ssm_c_re'], p['ssm_c_im'], p['ssm_d'])

    def heads(t, n):
        return t.reshape(t.shape[:2] + (n, HEAD_DIM))
    kh_c = rms_norm(heads(k_c, N_KV_HEADS), p['k_norm_g'])
    vh_c = heads(v_c, N_KV_HEADS)
    cos, sin = axial_rope(n_lat)
    qh_l = apply_rope(rms_norm(heads(q_l, N_Q_HEADS), p['q_norm_g']), cos, sin)
    kh_l = apply_rope(rms_norm(heads(k_l, N_KV_HEADS), p['k_norm_g']), cos, sin)
    vh_l = heads(v_l, N_KV_HEADS)
    ya_l = windowed_latent_attention(qh_l, kh_l, vh_l, kh_c, vh_c, p['attn_sinks'])

    yb_l = short_conv_mixer(cb_l, cc_l, cx_l, p['conv_w'])
    out_l = branch_merge(ys_l, yb_l, ya_l, gt_l, p)

    out_c = None
    if with_ctx_out:
        qh_c = rms_norm(heads(q_c, N_Q_HEADS), p['q_norm_g'])
        ya_c = context_attention(qh_c, kh_c, vh_c, p['attn_sinks'])
        yb_c = short_conv_mixer(cb_c, cc_c, cx_c, p['conv_w'])
        out_c = branch_merge(ys_c, yb_c, ya_c, gt_c, p)
    return out_c, out_l

def moe_ffn(h, w_router, b_router, w_gu, b_gu, w_down, b_down):
    n_tok, d = h.shape
    logits = (h @ w_router).astype(jnp.float32) + b_router.astype(jnp.float32)
    top_val, top_idx = lax.top_k(logits, TOP_K)
    gates = jax.nn.softmax(top_val, axis=-1)
    n_assign = n_tok * TOP_K
    flat_e = top_idx.reshape(-1)
    order = jnp.argsort(flat_e)
    sorted_e = flat_e[order]
    sorted_tok = (order // TOP_K).astype(jnp.int32)
    counts = jnp.zeros((N_EXPERTS,), jnp.int32).at[flat_e].add(1)
    padded = (counts + MOE_BLOCK - 1) // MOE_BLOCK * MOE_BLOCK
    pad_end = jnp.cumsum(padded)
    pad_start = pad_end - padded
    start = jnp.cumsum(counts) - counts
    slot = pad_start[sorted_e] + jnp.arange(n_assign, dtype=jnp.int32) - start[sorted_e]
    n_blocks = (n_assign + N_EXPERTS * (MOE_BLOCK - 1)) // MOE_BLOCK
    n_slots = n_blocks * MOE_BLOCK
    slot_tok = jnp.full((n_slots,), n_tok, jnp.int32).at[slot].set(sorted_tok)
    slot_gate = jnp.zeros((n_slots,), jnp.float32).at[slot].set(gates.reshape(-1)[order])
    block_expert = jnp.minimum(
        jnp.searchsorted(pad_end, jnp.arange(n_blocks, dtype=jnp.int32) * MOE_BLOCK, side='right'),
        N_EXPERTS - 1)
    h_pad = jnp.concatenate([h, jnp.zeros((1, d), h.dtype)], axis=0)

    def expert_block(args):
        tok, g, e = args
        gu = h_pad[tok] @ w_gu[e] + b_gu[e]
        glu = jnp.minimum(gu[:, 0::2], SWIGLU_LIMIT)
        up = jnp.clip(gu[:, 1::2], -SWIGLU_LIMIT, SWIGLU_LIMIT)
        act = glu * jax.nn.sigmoid(SWIGLU_ALPHA * glu) * (up + 1.0)
        y = act @ w_down[e] + b_down[e]
        return y * g[:, None].astype(y.dtype)

    ys = lax.map(expert_block, (slot_tok.reshape(n_blocks, MOE_BLOCK),
                                slot_gate.reshape(n_blocks, MOE_BLOCK), block_expert))
    out = jnp.zeros((n_tok + 1, d), ys.dtype).at[slot_tok].add(ys.reshape(n_slots, d))
    return out[:n_tok]

def hybrid_layer(x_c, x_l, c, c_ctx, p, with_ctx_out):
    mod_l = (jax.nn.silu(c) @ p['w_mod'] + p['b_mod'])[:, None, :]
    mod_c = (jax.nn.silu(c_ctx) @ p['w_mod'] + p['b_mod'])[None, None, :]
    sh1_l, sc1_l, g1_l, sh2_l, sc2_l, g2_l = jnp.split(mod_l, 6, axis=-1)
    sh1_c, sc1_c, g1_c, sh2_c, sc2_c, g2_c = jnp.split(mod_c, 6, axis=-1)
    h_l = modulate(rms_norm(x_l, p['norm1_g']), sh1_l, sc1_l)
    h_c = modulate(rms_norm(x_c, p['norm1_g']), sh1_c, sc1_c)
    mix_c, mix_l = hybrid_mixer(h_c, h_l, p, with_ctx_out)
    x_l = x_l + g1_l * mix_l
    h2_l = modulate(rms_norm(x_l, p['norm2_g']), sh2_l, sc2_l)
    if not with_ctx_out:
        y_l = moe_ffn(h2_l.reshape(-1, D_MODEL), p['w_router'], p['b_router'], p['w_gate_up'],
                      p['b_gate_up'], p['w_down'], p['b_down'])
        return x_c, x_l + g2_l * y_l.reshape(x_l.shape)
    x_c = x_c + g1_c * mix_c
    h2_c = modulate(rms_norm(x_c, p['norm2_g']), sh2_c, sc2_c)
    n_c = h2_c.shape[0] * h2_c.shape[1]
    tokens = jnp.concatenate([h2_c.reshape(-1, D_MODEL), h2_l.reshape(-1, D_MODEL)], axis=0)
    y = moe_ffn(tokens, p['w_router'], p['b_router'], p['w_gate_up'], p['b_gate_up'],
                p['w_down'], p['b_down'])
    x_c = x_c + g2_c * y[:n_c].reshape(x_c.shape)
    x_l = x_l + g2_l * y[n_c:].reshape(x_l.shape)
    return x_c, x_l

def setup_inputs(seed: int = 0) -> dict:
    key = jax.random.key(seed)
    ks = jax.random.split(key, 32)
    f32 = jnp.float32
    nl, d, g, st, gh = DEPTH, D_MODEL, N_SSM_GROUPS, SSM_STATE, SSM_GROUP

    def nrm(k, shape, scale):
        return jax.random.normal(k, shape, f32) * scale

    lam_im_init = jnp.pi * jnp.arange(st, dtype=f32)
    return {
        'x': nrm(ks[0], (BATCH, SEQ, d), 1.0),
        'c': nrm(ks[1], (BATCH, d), 1.0),
        'ctx': nrm(ks[2], (BATCH, CTX_LEN, d), 1.0),
        'c_ctx': nrm(ks[3], (d,), 1.0),
        'w_mod': nrm(ks[4], (nl, d, 6 * d), 0.5 * d ** -0.5),
        'b_mod': nrm(ks[5], (nl, 6 * d), 0.02),
        'norm1_g': 1.0 + nrm(ks[6], (nl, d), 0.05),
        'norm2_g': 1.0 + nrm(ks[7], (nl, d), 0.05),
        'w_in': nrm(ks[8], (nl, d, D_IN), d ** -0.5),
        'ssm_lam_re': -0.5 + nrm(ks[9], (nl, 2, g, st), 0.01),
        'ssm_lam_im': lam_im_init + nrm(ks[10], (nl, 2, g, st), 0.01),
        'ssm_log_dt': jax.random.uniform(ks[11], (nl, 2, g), f32, math.log(1e-3), math.log(1e-1)),
        'ssm_b_re': nrm(ks[12], (nl, 2, g, st, gh), (2 * gh) ** -0.5),
        'ssm_b_im': nrm(ks[13], (nl, 2, g, st, gh), (2 * gh) ** -0.5),
        'ssm_c_re': nrm(ks[14], (nl, 2, g, gh, st), st ** -0.5),
        'ssm_c_im': nrm(ks[15], (nl, 2, g, gh, st), st ** -0.5),
        'ssm_d': nrm(ks[16], (nl, D_SSM), 1.0),
        'w_glu': nrm(ks[17], (nl, D_SSM, D_SSM), D_SSM ** -0.5),
        'w_ssm_out': nrm(ks[18], (nl, D_SSM, d), D_SSM ** -0.5),
        'conv_w': nrm(ks[19], (nl, CONV_WIDTH, D_CONV), CONV_WIDTH ** -0.5),
        'w_conv_out': nrm(ks[20], (nl, D_CONV, d), D_CONV ** -0.5),
        'q_norm_g': 1.0 + nrm(ks[21], (nl, HEAD_DIM), 0.05),
        'k_norm_g': 1.0 + nrm(ks[22], (nl, HEAD_DIM), 0.05),
        'attn_sinks': nrm(ks[23], (nl, N_Q_HEADS), 1.0),
        'w_attn_out': nrm(ks[24], (nl, D_Q, d), D_Q ** -0.5),
        'w_o': nrm(ks[25], (nl, d, d), d ** -0.5),
        'w_router': nrm(ks[26], (nl, d, N_EXPERTS), d ** -0.5),
        'b_router': nrm(ks[27], (nl, N_EXPERTS), 0.01),
        'w_gate_up': nrm(ks[28], (nl, N_EXPERTS, d, 2 * D_EXPERT), d ** -0.5),
        'b_gate_up': nrm(ks[29], (nl, N_EXPERTS, 2 * D_EXPERT), 0.01),
        'w_down': nrm(ks[30], (nl, N_EXPERTS, D_EXPERT, d), D_EXPERT ** -0.5),
        'b_down': nrm(ks[31], (nl, N_EXPERTS, d), 0.01),
    }

def reference(x, c, ctx, c_ctx, w_mod, b_mod, norm1_g, norm2_g, w_in, ssm_lam_re, ssm_lam_im,
              ssm_log_dt, ssm_b_re, ssm_b_im, ssm_c_re, ssm_c_im, ssm_d, w_glu, w_ssm_out, conv_w,
              w_conv_out, q_norm_g, k_norm_g, attn_sinks, w_attn_out, w_o, w_router, b_router,
              w_gate_up, b_gate_up, w_down, b_down):
    x_c, x_l = ctx, x
    for l in range(DEPTH):
        p = {
            'w_mod': w_mod[l], 'b_mod': b_mod[l], 'norm1_g': norm1_g[l], 'norm2_g': norm2_g[l],
            'w_in': w_in[l],
            'ssm_lam_re': ssm_lam_re[l], 'ssm_lam_im': ssm_lam_im[l], 'ssm_log_dt': ssm_log_dt[l],
            'ssm_b_re': ssm_b_re[l], 'ssm_b_im': ssm_b_im[l], 'ssm_c_re': ssm_c_re[l],
            'ssm_c_im': ssm_c_im[l], 'ssm_d': ssm_d[l], 'w_glu': w_glu[l], 'w_ssm_out': w_ssm_out[l],
            'conv_w': conv_w[l], 'w_conv_out': w_conv_out[l],
            'q_norm_g': q_norm_g[l], 'k_norm_g': k_norm_g[l], 'attn_sinks': attn_sinks[l],
            'w_attn_out': w_attn_out[l], 'w_o': w_o[l],
            'w_router': w_router[l], 'b_router': b_router[l], 'w_gate_up': w_gate_up[l],
            'b_gate_up': b_gate_up[l], 'w_down': w_down[l], 'b_down': b_down[l],
        }
        x_c, x_l = hybrid_layer(x_c, x_l, c, c_ctx, p, l < DEPTH - 1)
    return x_l


_drawn_inputs = setup_inputs


def setup_inputs(seed=0):
    import zlib

    import numpy as np

    out = dict(_drawn_inputs(seed))
    spreads = {}
    factors = {'ctx': 3.92,
     'ssm_lam_re': 64.0,
     'ssm_lam_im': 34.304,
     'ssm_log_dt': 35.176,
     'ssm_b_re': 39.976,
     'ssm_b_im': 43.872,
     'ssm_c_re': 38.632,
     'ssm_c_im': 40.208,
     'q_norm_g': 8.0,
     'k_norm_g': 8.0,
     'attn_sinks': 8.0,
     'b_router': 6.297,
     'b_gate_up': 27.24,
     'b_down': 33.453}
    for name, (base, spread) in spreads.items():
        noise = np.random.default_rng([zlib.crc32(name.encode()), seed]).standard_normal(out[name].shape)
        drawn = base * np.exp(spread * noise) if base else spread * noise
        out[name] = jnp.asarray(drawn.astype(out[name].dtype))
    for name, factor in factors.items():
        out[name] = (out[name] * factor).astype(out[name].dtype)
    return out
```

```python
from contextlib import ExitStack
import math

import numpy as np

import concourse.bass as bass
from concourse import mybir

ALU = mybir.AluOpType
ACT = mybir.ActivationFunctionType
AX = mybir.AxisListType
F32 = mybir.dt.float32
I32 = mybir.dt.int32
U32 = mybir.dt.uint32

P = 128
D = 1024
KC = D // P
T = 256
TT = T // P
GRID_W = 64
HD, NQ, NKV = 64, 8, 2
NP = NQ // NKV
SG, SH, SS = 16, 16, 64
L = 8
NCH = 2 * T // L
CCH = NCH // 2
NE, F = 32, 1024
FC = F // P
NB = 64
EPS = 1e-6
LIMIT, ALPHA = 7.0, 1.702
NEG = -1e30
BANK = 512
TWO_PI = 2 * math.pi
PI_A = 6.28125
PI_B = float(np.float32(np.floor((TWO_PI - PI_A) * 2**20) / 2**20))
PI_C = float(np.float32(TWO_PI - PI_A - PI_B))
ROUND = 1.5 * 2**23
GELU_C, GELU_S = 0.044715, 2 * math.sqrt(2 / math.pi)

V_BMOD, V_N1, V_N2, V_C, V_CCTX, V_D, V_TAPS, V_ROWS = 0, 48, 56, 64, 72, 80, 82, 88


def build(nc, x, c, ctx, c_ctx, w_mod, b_mod, norm1_g, norm2_g, w_in, ssm_lam_re, ssm_lam_im,
          ssm_log_dt, ssm_b_re, ssm_b_im, ssm_c_re, ssm_c_im, ssm_d, w_glu, w_ssm_out, conv_w,
          w_conv_out, q_norm_g, k_norm_g, attn_sinks, w_attn_out, w_o, w_router, b_router,
          w_gate_up, b_gate_up, w_down, b_down, ident, before, iota, cosine, sine, window, out):
    with ExitStack() as stack:
        def sbuf(name, width, dtype=F32):
            return stack.enter_context(nc.sbuf_tensor(name, [P, width], dtype))

        even_w = sbuf("even_w", KC * 2 * F)
        odd_w = sbuf("odd_w", KC * 2 * F)
        down_w = sbuf("down_w", FC * D)
        toks = sbuf("toks", TT * D)
        hid = sbuf("hid", TT * D)
        wide = sbuf("wide", 4096)
        idn_t = sbuf("idn", P)
        bef_t = sbuf("bef", P)
        iota_t = sbuf("iota", NB)
        ones_t = sbuf("ones", P)
        silu_t = sbuf("silu", 3 * P)
        selgt_t = sbuf("selgt", 2 * T)
        act_a = sbuf("act_a", 512)
        act_t = sbuf("act_t", 512)
        ut_t = sbuf("ut", 1024)
        vec_t = sbuf("vec", V_ROWS)
        mod_t = sbuf("mod", 96)
        ab_t = sbuf("ab", 24)
        rt_t = sbuf("rt", 400)
        rt_i = sbuf("rt_i", 16, U32)
        qs_t = stack.enter_context(nc.sbuf_tensor("qs", [1, NE + 1], I32))

        def view(t, at, pattern, /, **sizes):
            n = 1
            for v in sizes.values():
                n *= v
            names = list(sizes)
            return t[:, at:at + n].rearrange(f"p ({' '.join(names)}) -> p {pattern or ' '.join(names)}", **sizes)

        GU = [view(even_w, 0, "", k=KC, n=2 * F), view(odd_w, 0, "", k=KC, n=2 * F)]
        DN = view(down_w, 0, "", k=FC, n=D)
        X = view(toks, 0, "", t=TT, d=D)
        H2 = view(hid, 0, "", t=TT, d=D)
        CX = H2
        ZS = view(hid, 0, "", r=2, g=SG, c=NCH)
        ZR = view(even_w, 15360, "", r=2, g=SG, c=CCH)
        SCT = [even_w[:, 1024:1536], even_w[:, 1536:2048]]
        HT = view(wide, 0, "", k=KC, t=2 * T)
        H2T = view(wide, 0, "", k=KC, t=T)
        BROW = wide[:, 2048:4096]
        GS, XG, GL, UP = wide[:, 0:512], view(wide, 512, "", c=4, n=P), wide[:, 1024:1536], wide[:, 1536:2048]
        IDN, BEF, IOTA, ONES = idn_t[:, :], bef_t[:, :], iota_t[:, :], ones_t[:, :]
        SILU = view(silu_t, 0, "", k=KC, m=32)
        SELG = view(silu_t, 0, "", t=TT, m=3 * NB)
        COS, SIN = view(act_a, 320, "", t=TT, d=32), view(act_a, 384, "", t=TT, d=32)
        SEL = view(rt_t, 0, "", t=TT, n=NB)
        SELGT = view(selgt_t, 0, "", h=2, t=T)
        ACTA, ACTT = act_a, view(act_t, 0, "", c=4, n=P)
        UT = view(ut_t, 0, "", m=2, t=2 * T)
        G2ROW = ut_t
        VEC = vec_t
        MOD = view(mod_t, 0, "", w=6, k=KC, v=2)
        A1 = view(ab_t, 0, "", k=KC, v=2)
        A2 = ab_t[:, 16:24]

        LG, MK, GM, TE = (view(rt_t, 64 * i, "", t=TT, e=NE) for i in range(4))
        PM = view(rt_t, 256, "", t=TT, e=NE)
        V8, I8F, E4, G4 = (view(rt_t, 320 + 16 * i, "", t=TT, n=8) for i in range(4))
        NV0, ESUM, ERCP, CNT, NBK, C1 = (rt_t[:, 384 + 2 * i:386 + 2 * i] for i in range(6))
        NBK, CNT, C1 = NBK[:, 0:1], CNT[:, 0:1], C1[:, 0:1]
        I8 = view(rt_i, 0, "", t=TT, n=8)
        STAT = rt_t[:, 320:384]
        GT = act_a
        PAR, PAI = (view(down_w, 7808 + 160 * i, "", k=5, r=2, g=SG) for i in range(2))
        PA = view(selgt_t, 256, "", r=2, k=8, g=SG)
        QST = rt_t[:, 64:136]
        AC = view(rt_t, 160, "", b=2, n=12)
        SINKS = act_a[:, 448:456]
        SIG16 = act_a[:, 496:512]
        YT1, YG = even_w[:, 2048:2560], even_w[:, 2560:3072]
        W1N = view(even_w, 0, "", r=2, g=SG, j=L, h=SH)
        MZ = view(down_w, 2048, "", g=SG, j=P)
        UC = view(even_w, 0, "", g=SG, j=L, h=SH)
        YC = view(even_w, 0, "", j=L, d=T)
        U2 = view(even_w, 2048, "", g=SG, c=NCH)
        YS, YA = view(even_w, 3072, "", m=2, t=T), view(even_w, 3584, "", m=2, t=T)
        W1T = view(even_w, 4096, "", r=2, g=SG, s=P)
        TMP = [view(even_w, 4096 + 2048 * i, "", g=SG, j=L, h=SH) for i in range(2)]
        CM = view(even_w, 8192, "", r=2, g=SG, j=P)
        CMV = view(even_w, 8192, "", r=2, g=SG, j=L, h=SH)
        TZ = view(even_w, 12288, "", g=SG, j=P)
        QP = view(even_w, 14336, "", t=TT, i=NP + 1, d=P)
        BB = view(even_w, 14336, "", r=2, g=SG, z=2, h=SH)
        BBV = BB
        BP = view(even_w, 14336 + 1024, "", r=2, g=SG, h=SH)
        YCONV = view(act_t, 0, "", m=2, t=T)
        CT = view(even_w, 15872, "", r=2, g=SG, h=SH)
        BRAW = view(down_w, 5632, "", r=2, g=SG, h=SH)
        CRAW = view(down_w, 6144, "", r=2, a=2, s=P)
        LRAW = rt_t[0:SG, 0:256].rearrange("p (r s) -> p r s", r=2)
        LAM = view(act_a, 0, "", n=20, g=SG)
        POW = view(selgt_t, 0, "", r=2, k=L, g=SG)
        EXPO = view(selgt_t, 256, "", r=2, j=L, g=SG)
        SSMO = view(even_w, 4096, "", k=2, n=D)
        CONVO = view(even_w, 6144, "", k=2, n=D)
        ATTO = view(even_w, 8192, "", k=NP, n=D)
        MERG = view(even_w, 12288, "", k=KC, t=T)
        VROWS = down_w[:, 8064:8192]
        MODR = [act_t[:, :], down_w[:, 5632:6144], down_w[:, 6144:6656]]
        DG = view(odd_w, 8192, "", n=4, c=P)
        XN = view(down_w, 0, "", t=4, d=D)
        QK = view(down_w, 0, "", t=TT, h=NQ + NKV, d=HD)
        YAT = view(down_w, 0, "", i=NP, t=T)
        KCX = view(down_w, 1280, "", t=TT, h=NKV, d=HD)
        VV = view(down_w, 1536, "", c=4, d=P)
        QT = view(down_w, 2048, "", i=NP, t=T)
        KT = view(down_w, 3072, "", g=2, t=2 * T)
        PR = view(down_w, 4096, "", b=2, h=2, k=BANK)
        BCX = view(down_w, 4096, "", i=6, t=T)
        PT = view(even_w, 0, "", c=4, q=2 * P)
        GSG = view(down_w, 2048, "", b=2, s=3, t=T)
        QKG = view(down_w, 7680, "", q=2, d=HD)
        MASK = view(down_w, 6656, "", t=TT, k=BANK)
        WR = view(down_w, 7680, "", k=KC, e=NE)
        BR = down_w[:, 7936:7968]
        BDN = down_w[0:NE, 2048:3072]
        G1ROW, A2ROW, S2ROW = down_w[:, 3072:4096], down_w[:, 4096:5120], down_w[:, 5120:6144]
        WGLU = view(odd_w, 6144, "", k=2, n=T)

        names = """small x_ld ctx_ld const ssm_ld c_ld lam_ld braw_ld bmod_ld qk_ld
            ra_ld rb_ld sq_sum sd_ok sd2 wglu_ld br_ld gu_ld0 gu_ld1 dn_ld router_ld mask_ld bd_ld
            vec_ld vec_t vec_ok ones silu_ok silu2 mod_pe modr_ok modt_pe mod_ok stat_ok xn_ok xnt_pe ht_ok_a ht_ok_v
            cx_used xn_used ra_free rb_free
            lam_t lam_ok ct_t ct_ok dt_ok lamtmp tabs_ok w1t_pe w1t_ok mz_pe mz_ok tz_zero tz_ld bwd0
            u_pe ut_ok bcx_pe bcx_ok kcx_pe kcx_ok qk_pe qk_ok yconv_ok
            uc_pe uc_ok u2_pe u2_ok inc_pe zs_ok scan_ok zr_ok y_pe yc_ok yt_pe ys_ok gelu_in gelu_sg z_ok glu_pe glu_ok yssm_ok
            qss qrs qp_ok qt_pe qt_ok kt_z s_pe s_ok smax sexp p_ok p_done pt_pe pt_ok pv_pe yat_ok
            g_pe g_sg merg_ok merge_done wo_pe row_pe row_ok x1_ok ss2 ss2_ok h2_ok h2t_pe h2t_ok
            rt_pe ex_in ex_out mk_ok pos_pe tab qs_pe qs_ok acc0
            sel gathered selgt gs xt xg gup glu sg actm act atp at dnp yc scat shift
            dve act_s pool fin out_s ssmo_ld dgk xn_t_free""".split()
        S = {n: stack.enter_context(nc.semaphore("s_" + n)) for n in names}
        PS = stack.enter_context(nc.psum_tensor("ps", [P, 8, BANK], F32))
        block = stack.enter_context(nc.Block())

        w_mod_v = w_mod[0].rearrange("(k p) n -> p k n", p=P)
        w_in_v = w_in[0].rearrange("(k p) n -> p k n", p=P)
        RA = view(odd_w, 0, "", k=KC, n=1024)
        RB = view(odd_w, 8192, "", k=KC, n=1024)
        RAM, RBM = view(odd_w, 0, "", k=4, n=2048), view(odd_w, 8192, "", k=4, n=2048)
        RAG, RBG = view(odd_w, 0, "", k=KC, s=3, n=T), view(odd_w, 8192, "", k=KC, s=3, n=T)

        @block.sync
        def _(sp):
            def load(dst, src, name):
                sp.dma_start(dst, src).then_inc(S[name], 16)
            for k in range(4):
                load(RAM[:, k, :], w_mod_v[:, k, 0:2048], "ra_ld")
            for k in range(4):
                load(RBM[:, k, :], w_mod_v[:, 4 + k, 0:2048], "rb_ld")
            sp.wait_ge(S["ra_free"], 1)
            load(RA, w_in_v[:, :, 0:1024], "ra_ld")
            sp.wait_ge(S["rb_free"], 1)
            load(view(odd_w, 8192, "", k=KC, n=768), w_in_v[:, :, 1024:1792], "rb_ld")
            for third in (1, 2):
                sp.wait_ge(*((S["bcx_pe"], 6) if third == 1 else (S["ra_free"], 2)))
                for k in range(4):
                    load(RAM[:, k, :], w_mod_v[:, k, third * 2048:(third + 1) * 2048], "ra_ld")
                sp.wait_ge(*((S["qk_pe"], TT) if third == 1 else (S["rb_free"], 2)))
                for k in range(4):
                    load(RBM[:, k, :], w_mod_v[:, 4 + k, third * 2048:(third + 1) * 2048], "rb_ld")
            for m in range(4):
                R, r = (RAG, "ra") if m % 2 == 0 else (RBG, "rb")
                sp.wait_ge(*((S[r + "_free"], 3) if m < 2 else (S["g_pe"], 4 * m - 5)))
                for s in range(3):
                    load(R[:, :, s, :], w_in_v[:, :, 1792 + s * D + m * T:1792 + s * D + (m + 1) * T], r + "_ld")
                if m == 0:
                    load(WGLU, w_glu[0].rearrange("(k p) n -> p k n", p=P), "wglu_ld")
                if m == 1:
                    sp.wait_ge(S["y_pe"], 1)
                    load(SSMO, w_ssm_out[0].rearrange("(k p) n -> p k n", p=P), "br_ld")
                    load(CONVO, w_conv_out[0].rearrange("(k p) n -> p k n", p=P), "br_ld")
                    for g in range(NKV):
                        load(ATTO[g * HD:(g + 1) * HD], w_attn_out[0, g * NP * HD:(g + 1) * NP * HD].rearrange("(i d) n -> d i n", d=HD), "br_ld")
            sp.wait_ge(S["g_pe"], 11)
            load(RA, w_o[0].rearrange("(k p) n -> p k n", p=P), "ra_ld")
            sp.wait_ge(S["merge_done"], 1)
            load(WR, w_router[0].rearrange("(k p) e -> p k e", p=P), "router_ld")
            load(BR[0:1, :], b_router, "router_ld")
            load(BDN, b_down[0], "bd_ld")

            def load_gu(par, e):
                for k in range(0, KC, 2):
                    load(GU[par][:, k:k + 2, :], w_gate_up[0, e, k * P:(k + 2) * P, :].rearrange("a (k p) n -> p (a k) n", p=P), f"gu_ld{par}")
                load(BROW[32 * par:32 * par + 1, :], b_gate_up[0, e, :], f"gu_ld{par}")

            def load_dn(e):
                for k in range(0, FC, 4):
                    load(DN[:, k:k + 4, :], w_down[0, e, k * P:(k + 4) * P, :].rearrange("a (k p) n -> p (a k) n", p=P), "dn_ld")

            sp.wait_ge(S["wo_pe"], 1)
            sp.wait_ge(S["yssm_ok"], 1)
            load_gu(0, slice(0, 1))
            sp.wait_ge(S["acc0"], 1)
            sp.wait_ge(S["h2_ok"], TT)
            sp.wait_ge(S["mk_ok"], 1)
            load_dn(slice(0, 1))
            load_gu(1, slice(1, 2))
            sp.wait_ge(S["qs_ok"], 1)
            done = sp.value_load(qs_t[0:1, 1:2], min_val=1, max_val=4 * NE)
            sp.wait_ge(S["dnp"], done)
            load_dn(slice(1, 2))
            with sp.Fori(1, NE // 2) as pair:
                for par in range(2):
                    e = pair * 2 + par
                    two_ago = sp.value_load(qs_t[0:1, bass.ds(e - 1, 1)], min_val=1, max_val=4 * NE)
                    last_one = sp.value_load(qs_t[0:1, bass.ds(e, 1)], min_val=1, max_val=4 * NE)
                    sp.wait_ge(S["gup"], two_ago * 2)
                    load_gu(par, bass.ds(e, 1))
                    sp.wait_ge(S["dnp"], last_one)
                    load_dn(bass.ds(e, 1))
            sp.wait_ge(S["fin"], 1)
            sp.dma_start(out[0].rearrange("(t p) d -> p t d", p=P), X).then_inc(S["out_s"], 16)
            sp.wait_ge(S["out_s"], 16)

        @block.tensor
        def _(pe):
            mm, tp = pe.matmul, pe.transpose

            def need(name, n=1):
                pe.wait_ge(S[name], n)

            need("const", 48)
            need("vec_ld", 16 * 7)
            tp(PS[:, 7, 0:V_ROWS], VROWS[0:V_ROWS, :], IDN[0:V_ROWS, 0:V_ROWS]).then_inc(S["vec_t"], 1)
            need("lam_ld", 64)
            for r in range(2):
                last = tp(PS[:, 6, r * SG:(r + 1) * SG], LRAW[:, r, :], IDN[0:SG, 0:SG])
            last.then_inc(S["lam_t"], 1)
            need("c_ld", 128)
            for r in range(2):
                for a in range(2):
                    last = tp(PS[:, 5, (r * 2 + a) * P:(r * 2 + a + 1) * P], CRAW[:, r, a, :], IDN)
            last.then_inc(S["ct_t"], 1)

            def modulation(third, bank):
                for k in range(KC):
                    R, r = (RAM, "ra") if k < 4 else (RBM, "rb")
                    if k % 4 == 0:
                        need(r + "_ld", (64, 144, 208)[third])
                    for q in range(4):
                        last = mm(PS[32 * q:32 * q + 32, bank, :], SILU[:, k, :], R[:, k % 4, q * BANK:(q + 1) * BANK],
                                  start=(k == 0), stop=(k == KC - 1), tile_position=(0, 32 * q))
                    if k == 3:
                        last.then_inc(S["ra_free"], 1)
                last.then_inc(S["rb_free"], 1)

            def modulation_columns(third, bank):
                need("modr_ok", third + 1)
                for cc in range(4):
                    last = tp(PS[:, bank, cc * P:(cc + 1) * P], MODR[third][:, cc * P:(cc + 1) * P], IDN)
                last.then_inc(S["modt_pe"], 1)

            need("silu2")
            modulation(0, 4)
            need("xn_ok", 4)
            for k in range(KC):
                if k >= 4:
                    need("ht_ok_a" if k % 2 == 0 else "ht_ok_v", (k - 4) // 2 + 1)
                for t in range(4):
                    last = tp(PS[:, k % 4, t * P:(t + 1) * P], XN[:, t, k * P:(k + 1) * P], IDN)
                last.then_inc(S["xnt_pe"], 1)
                if k == 3:
                    need("lam_ok"); need("ct_ok")
                    modulation_columns(0, 5)
            need("ht_ok_a", 4)
            need("ht_ok_v", 4)
            need("ra_ld", 80)
            for m in range(2):
                for k in range(KC):
                    last = mm(PS[:, 6 + m, :], RA[:, k, m * P:(m + 1) * P], HT[:, k, :], start=(k == 0), stop=(k == KC - 1))
                last.then_inc(S["u_pe"], 1)
            for i in range(6):
                if i >= 4:
                    need("bcx_ok", i - 3)
                for k in range(KC):
                    last = mm(PS[:, i % 4, 0:T], RA[:, k, T + i * P:T + (i + 1) * P], HT[:, k, T:2 * T], start=(k == 0), stop=(k == KC - 1))
                last.then_inc(S["bcx_pe"], 1)
            RQ = view(odd_w, 8192, "", k=KC, n=768)
            need("rb_ld", 80)
            for t in range(TT):
                for k in range(KC):
                    last = mm(PS[:, 4, t * T:(t + 1) * T], HT[:, k, t * P:(t + 1) * P], RQ[:, k, 512:768], start=(k == 0), stop=(k == KC - 1))
            last.then_inc(S["kcx_pe"], 1)
            need("ut_ok", 2)
            need("bcx_ok", 6)
            for t in range(TT):
                for k in range(KC):
                    mm(PS[:, 6 + t, :], HT[:, k, T + t * P:T + (t + 1) * P], RQ[:, k, 0:512], start=(k == 0), stop=(k == KC - 1))
                    last = mm(PS[:, 5, t * T:(t + 1) * T], HT[:, k, T + t * P:T + (t + 1) * P], RQ[:, k, 512:768], start=(k == 0), stop=(k == KC - 1))
                last.then_inc(S["qk_pe"], 1)
            need("bcx_ok", 6)
            for j in range(L):
                for m in range(2):
                    last = tp(PS[0:NCH, j // 2, (j % 2) * T + m * P:(j % 2) * T + (m + 1) * P], UT[:, m, j::L], IDN)
            last.then_inc(S["uc_pe"], 1)
            need("tabs_ok", 1)
            need("qk_ok", 4)
            need("kcx_ok", 2)
            for n in range(8):
                if n >= 4:
                    need("w1t_ok", n - 3)
                for i in range(4):
                    last = tp(PS[:, 4 + n % 4, i * P:(i + 1) * P], W1N[:, n // 4, (n % 4) * 4 + i, :, :].rearrange("p j h -> p (j h)"), IDN)
                last.then_inc(S["w1t_pe"], 1)
            need("uc_ok", 1)
            for g in range(SG):
                for r in range(2):
                    last = mm(PS[0:2 * SH, g // 4, (g % 4) * P:(g % 4 + 1) * P], BB[:, r, g, :, :].rearrange("p z h -> p (z h)"), CM[:, r, g, :], start=(r == 0), stop=(r == 1))
            last.then_inc(S["mz_pe"], 1)
            need("w1t_ok", 8)
            for g in range(SG):
                last = tp(PS[:, 4 + g // 8, (g % 8) * NCH:(g % 8 + 1) * NCH], UC[0:NCH, g, :, :].rearrange("p j h -> p (j h)"), IDN[0:NCH, 0:NCH])
            last.then_inc(S["u2_pe"], 1)
            need("u2_ok", 1)
            need("mz_ok", 1)
            for r in range(2):
                for g in range(SG):
                    last = mm(PS[:, r * 2 + g // 8, (g % 8) * NCH:(g % 8 + 1) * NCH], W1T[:, r, g, :], U2[:, g, :], start=True, stop=True)
            last.then_inc(S["inc_pe"], 1)
            modulation(1, 4)
            modulation(2, 6)
            modulation_columns(1, 5)
            modulation_columns(2, 7)
            need("qp_ok", 1)
            need("mod_ok", 3)
            for t in range(TT):
                for i in range(NP):
                    last = tp(PS[:, 4 + i // 2, (i % 2) * T + t * P:(i % 2) * T + (t + 1) * P], QP[:, t, i, :], IDN)
            for t in range(TT):
                last = tp(PS[:, 6, T + t * P:T + (t + 1) * P], QP[:, t, NP, :], IDN)
            for t in range(TT):
                last = tp(PS[:, 6, t * P:(t + 1) * P], KCX[:, t, :, :].rearrange("p h d -> p (h d)"), IDN)
            last.then_inc(S["qt_pe"], 1)

            def attend(n):
                need("p_ok", n + 1)
                if n:
                    need("pt_ok", n)
                for kc in range(4):
                    for g in range(2):
                        last = tp(PS[:, 4 + kc // 2, (kc % 2) * T + g * P:(kc % 2) * T + (g + 1) * P], PR[:, n % 2, g, kc * P:(kc + 1) * P], IDN)
                last.then_inc(S["pt_pe"], 1)
                need("pt_ok", n + 1)
                if n >= 2:
                    need("yat_ok", n - 1)
                for kc in range(4):
                    for g in range(2):
                        last = mm(PS[g * HD:(g + 1) * HD, 6 + n % 2, 0:P], VV[:, kc, g * HD:(g + 1) * HD], PT[:, kc, g * P:(g + 1) * P], start=(kc == 0), stop=(kc == 3), tile_position=(0, g * HD))
                last.then_inc(S["pv_pe"], 1)

            need("qt_ok", 2)
            need("zs_ok", 2)
            for n in range(2 * NP):
                t, i = n // NP, n % NP
                if n >= 2:
                    need("s_ok", n - 1)
                for g in range(2):
                    last = mm(PS[:, 2 * (n % 2) + g, :], QT[:, i, t * P:(t + 1) * P], KT[:, g, :], start=True, stop=True)
                last.then_inc(S["s_pe"], 1)
                if n:
                    attend(n - 1)
            attend(2 * NP - 1)
            need("zr_ok", 1)
            need("tz_ld", 16 * 15)
            need("s_ok", 2 * NP)
            for g in range(SG):
                o = PS[0:CCH, g // 4, (g % 4) * P:(g % 4 + 1) * P]
                mm(o, U2[:, g, CCH:NCH], TZ[:, g, :], start=True, stop=False)
                mm(o, ZR[:, 0, g, :], CM[:, 0, g, :], start=False, stop=False)
                last = mm(o, ZR[:, 1, g, :], CM[:, 1, g, :], start=False, stop=True)
            last.then_inc(S["y_pe"], 1)
            need("yc_ok", 1)
            need("pt_ok", 2 * NP)
            for m in range(2):
                for j in range(L):
                    last = tp(PS[:, 4, m * T + j * CCH:m * T + (j + 1) * CCH], YC[0:CCH, j, m * P:(m + 1) * P], IDN[0:CCH, 0:CCH])
            last.then_inc(S["yt_pe"], 1)
            need("z_ok", 1)
            need("wglu_ld", 16)
            for m in range(2):
                for k in range(2):
                    last = mm(PS[:, 5, m * T:(m + 1) * T], WGLU[:, k, m * P:(m + 1) * P], YS[:, k, :], start=(k == 0), stop=(k == 1))
            last.then_inc(S["glu_pe"], 1)
            need("br_ld", 64)
            need("yssm_ok", 1)
            need("yat_ok", 2 * NP)
            need("yconv_ok", 1)
            for m in range(KC):
                R, r = (RAG, "ra") if (m // 2) % 2 == 0 else (RBG, "rb")
                if m % 2 == 0:
                    need(r + "_ld", 256 if m < 4 else 304)
                if m >= 2:
                    need("merg_ok", m - 1)
                b = 4 * (m % 2)
                for s in range(3):
                    o = PS[:, b + s // 2, (s % 2) * T:(s % 2 + 1) * T]
                    for k in range(KC):
                        last = mm(o, R[:, k, s, (m % 2) * P:(m % 2 + 1) * P], HT[:, k, T:2 * T], start=(k == 0), stop=(k == KC - 1))
                last.then_inc(S["g_pe"], 1)
                for k in range(2):
                    mm(PS[:, b + 2, 0:T], SSMO[:, k, m * P:(m + 1) * P], YA[:, k, :], start=(k == 0), stop=(k == 1))
                for k in range(2):
                    mm(PS[:, b + 2, T:2 * T], CONVO[:, k, m * P:(m + 1) * P], YCONV[:, k, :], start=(k == 0), stop=(k == 1))
                for k in range(NP):
                    last = mm(PS[:, b + 3, 0:T], ATTO[:, k, m * P:(m + 1) * P], YAT[:, k, :], start=(k == 0), stop=(k == NP - 1))
                last.then_inc(S["g_pe"], 1)
            need("merg_ok", KC)
            need("ra_ld", 320)
            for t in range(TT):
                for h in range(2):
                    for k in range(KC):
                        last = mm(PS[:, 2 * t + h, :], MERG[:, k, t * P:(t + 1) * P], RA[:, k, h * BANK:(h + 1) * BANK], start=(k == 0), stop=(k == KC - 1))
            last.then_inc(S["wo_pe"], 1)
            for row in range(4):
                if row >= 2:
                    need("row_ok", row - 1)
                for k in range(KC):
                    need("dgk", row * KC + k + 1)
                    last = mm(PS[:, 4 + 2 * (row % 2) + k // 4, (k % 4) * P:(k % 4 + 1) * P], ONES, DG[:, (row * KC + k) % 4, :], start=True, stop=True)
                    last.then_inc(S["row_pe"], 1)
            need("h2_ok", TT)
            need("row_ok", 4)
            for t in range(TT):
                for k in range(KC):
                    last = tp(PS[:, k // 2, (k % 2) * T + t * P:(k % 2) * T + (t + 1) * P], H2[:, t, k * P:(k + 1) * P], IDN)
            last.then_inc(S["h2t_pe"], 1)
            need("h2t_ok", 1)
            need("router_ld", 32)
            for t in range(TT):
                for k in range(KC):
                    mm(PS[:, 6, t * 64:t * 64 + NE], H2T[:, k, t * P:(t + 1) * P], WR[:, k, :], start=(k == 0), stop=False)
                last = mm(PS[:, 6, t * 64:t * 64 + NE], ONES[0:1, :], BR[0:1, :], start=False, stop=True)
            last.then_inc(S["rt_pe"], 1)
            need("mk_ok", 1)
            mm(PS[:, 7, 0:NE], BEF, MK[:, 0, :], start=True, stop=True)
            mm(PS[:, 7, 64:64 + NE], ONES, MK[:, 0, :], start=True, stop=False)
            mm(PS[:, 7, 64:64 + NE], BEF, MK[:, 1, :], start=False, stop=True)
            mm(PS[0:NE, 7, 128:129], MK[:, 0, :], ONES[:, 0:1], start=True, stop=False)
            mm(PS[0:NE, 7, 128:129], MK[:, 1, :], ONES[:, 0:1], start=False, stop=True)
            for t in range(TT):
                last = tp(PS[0:NE, 7, 256 + t * P:256 + (t + 1) * P], GM[:, t, :], IDN)
            last.then_inc(S["pos_pe"], 1)
            need("tab", 1)
            mm(PS[0:1, 6, 0:NE + 1], NBK[0:NE, :], BEF[0:NE, 0:NE + 1], start=True, stop=True).then_inc(S["qs_pe"], 1)
            need("bd_ld", 16)
            for t in range(TT):
                for h in range(2):
                    last = mm(PS[:, 2 * t + h, :], GT[0:NE, t * P:(t + 1) * P], BDN[:, h * BANK:(h + 1) * BANK], start=True, stop=True)
            last.then_inc(S["acc0"], 1)
            need("qs_ok", 1)
            with pe.Fori(0, NE // 2) as pair:
                for par in range(2):
                    e = pair * 2 + par
                    first = pe.value_load(qs_t[0:1, bass.ds(e, 1)], min_val=0, max_val=4 * NE)
                    end = pe.value_load(qs_t[0:1, bass.ds(e + 1, 1)], min_val=1, max_val=4 * NE)
                    with pe.Fori(first, end) as q:
                        pe.wait_ge(S["sel"], q + 1)
                        for t in range(TT):
                            for h in range(2):
                                last = mm(PS[h * NB:(h + 1) * NB, 6, :], SEL[:, t, :], H2[:, t, h * BANK:(h + 1) * BANK], start=(t == 0), stop=(t == 1))
                        last.then_inc(S["gathered"], 1)
                        for h in range(2):
                            for t in range(TT):
                                last = tp(PS[:, 5, h * T + t * P:h * T + (t + 1) * P], SELG[:, t, (1 - h) * NB:(1 - h) * NB + P], IDN)
                        last.then_inc(S["selgt"], 1)
                        pe.wait_ge(S["gs"], q + 1)
                        for i in range(4):
                            last = tp(PS[:, 7, i * P:(i + 1) * P], GS[:, i * P:(i + 1) * P], IDN)
                        last.then_inc(S["xt"], 1)
                        pe.wait_ge(S["xg"], 2 * (q + 1))
                        pe.wait_ge(S[f"gu_ld{par}"], (pair + 1) * 80)

                        def gate_up(j, ks):
                            for k in ks:
                                for h in range(2):
                                    mm(PS[h * NB:(h + 1) * NB, 4 + j, :], XG[:, k % 4, (k // 4) * NB:(k // 4 + 1) * NB],
                                       GU[par][:, k, h * F + j * BANK:h * F + (j + 1) * BANK], start=(k == 0), stop=False)

                        def gate_up_bias(j):
                            for h in range(2):
                                last = mm(PS[h * NB:(h + 1) * NB, 4 + j, :], ONES[32 * par:32 * par + 1, 0:NB],
                                          BROW[32 * par:32 * par + 1, h * F + j * BANK:h * F + (j + 1) * BANK], start=False, stop=True)
                            last.then_inc(S["gup"], 1)

                        def act_turned(j, bank):
                            pe.wait_ge(S["act"], 2 * q + j + 1)
                            for i in range(2):
                                last = tp(PS[:, bank, i * P:(i + 1) * P], ACTA[:, j * T + i * P:j * T + (i + 1) * P], IDN)
                            last.then_inc(S["atp"], 1)

                        def down(j):
                            pe.wait_ge(S["at"], 2 * q + j + 1)
                            for i in range(2):
                                for hh in range(2):
                                    for h in range(2):
                                        last = mm(PS[h * NB:(h + 1) * NB, 6, :], ACTT[:, 2 * j + i, hh * NB:(hh + 1) * NB],
                                                  DN[:, hh * 4 + 2 * j + i, h * BANK:(h + 1) * BANK],
                                                  start=(j + i + hh == 0), stop=(j + i + hh == 3))
                            return last

                        gate_up(0, range(KC))
                        gate_up_bias(0)
                        gate_up(1, range(4))
                        act_turned(0, 7)
                        gate_up(1, range(4, KC))
                        gate_up_bias(1)
                        pe.wait_ge(S["dn_ld"], (e + 1) * 32)
                        down(0)
                        act_turned(1, 4)
                        down(1).then_inc(S["dnp"], 1)
                        pe.wait_ge(S["yc"], q + 1)
                        for t in range(TT):
                            for h in range(2):
                                last = mm(PS[:, 2 * t + h, :], SELGT[:, h, t * P:(t + 1) * P], GS, start=False, stop=True, skip_group_check=True)
                        last.then_inc(S["scat"], 1)

        @block.scalar
        def _(act):
            n = [0]

            def do(ins):
                n[0] += 1
                return ins.then_inc(S["act_s"], 1)

            def settle():
                act.wait_ge(S["act_s"], n[0])

            def tell(name, k=1):
                settle()
                act.sem_inc(S[name], k)

            def need(name, k=1):
                act.wait_ge(S[name], k)

            def load(dst, src, name):
                act.dma_start(dst, src).then_inc(S[name], 16)

            def copy(dst, src):
                return do(act.activation(dst, src, ACT.Copy))

            for t in range(TT):
                load(CX[:, t, :], ctx[0, t * P:(t + 1) * P, :], "x_ld")
                load(X[:, t, :], x[0, t * P:(t + 1) * P, :], "x_ld")
            for z in range(2):
                load(LAM[z * SS:(z + 1) * SS, 0, :], ssm_log_dt[0, z:z + 1, :].to_broadcast([SS, SG]), "lam_ld")
            for r, v in enumerate((ssm_lam_re, ssm_lam_im)):
                load(LRAW[:, r, :].rearrange("g (z s) -> g z s", z=2), v[0].rearrange("z g s -> g z s"), "lam_ld")
            load(SINKS, attn_sinks.to_broadcast([P, NQ]), "qk_ld")
            load(QKG[:, 0, :], q_norm_g.to_broadcast([P, HD]), "qk_ld")
            load(QKG[:, 1, :], k_norm_g.to_broadcast([P, HD]), "qk_ld")
            load(COS, cosine.rearrange("(t p) d -> p t d", p=P), "qk_ld")
            load(SIN, sine.rearrange("(t p) d -> p t d", p=P), "qk_ld")
            load(MASK, window.rearrange("(t p) k -> p t k", p=P), "mask_ld")
            need("vec_ok")
            do(act.activation(SIG16, VEC[:, V_C:V_C + 16], ACT.Sigmoid))
            tell("silu_ok")
            need("lam_ld", 64)
            do(act.activation(LAM[:, 1, :], LAM[:, 0, :], ACT.Exp))
            tell("dt_ok")
            need("x_ld", 64)
            for i, src in enumerate((CX[:, 0, :], CX[:, 1, :], X[:, 0, :], X[:, 1, :])):
                do(act.activation(XN[:, i, :], src, ACT.Square, accum_out=STAT[:, i:i + 1]))
            tell("sq_sum")
            need("sd_ok")
            do(act.activation(STAT[:, 8:12], STAT[:, 4:8], ACT.Sqrt))
            tell("stat_ok")

            def modulation_row(third, bank):
                need("rb_free", third + 1)
                copy(MODR[third], PS[:, bank, :])
                tell("modr_ok")

            modulation_row(0, 4)
            need("mod_ok", 1)
            for k in range(0, KC, 2):
                need("xnt_pe", k + 1)
                do(act.activation(HT[:, k, T:2 * T], PS[:, k % 4, T:2 * T], ACT.Identity, bias=MOD[:, 0, k, 0:1], scale=A1[:, k, 0:1]))
                do(act.activation(HT[:, k, 0:T], PS[:, k % 4, 0:T], ACT.Identity, bias=MOD[:, 0, k, 1:2], scale=A1[:, k, 1:2]))
                tell("ht_ok_a")
            for m in range(2):
                need("u_pe", m + 1)
                copy(UT[:, m, :], PS[:, 6 + m, :])
                tell("ut_ok")
            for i in range(6):
                need("bcx_pe", i + 1)
                copy(BCX[:, i, :], PS[:, i % 4, 0:T])
                tell("bcx_ok")
            need("kcx_pe")
            need("xnt_pe", KC)
            kv = PS[:, 4, :].rearrange("p (t n) -> p t n", t=TT)
            copy(KCX[:, :, :, :].rearrange("p t h d -> p t (h d)"), kv[:, :, 0:P])
            tell("kcx_ok")
            copy(VV[:, 0:2, :], kv[:, :, P:2 * P])
            tell("kcx_ok")
            for t in range(TT):
                need("qk_pe", t + 1)
                copy(QK[:, t, 0:NQ, :].rearrange("p (i g) d -> p g i d", g=2), PS[:, 6 + t, :].rearrange("p (g i d) -> p g i d", g=2, i=NP))
                tell("qk_ok")
            kv = PS[:, 5, :].rearrange("p (t n) -> p t n", t=TT)
            copy(QK[:, :, NQ:NQ + NKV, :].rearrange("p t h d -> p t (h d)"), kv[:, :, 0:P])
            copy(VV[:, 2:4, :], kv[:, :, P:2 * P])
            tell("qk_ok", 2)
            for i in range(8):
                need("w1t_pe", i + 1)
                copy(W1T[:, i // 4, (i % 4) * 4:(i % 4) * 4 + 4, :].rearrange("p g s -> p (g s)"), PS[:, 4 + i % 4, :])
                tell("w1t_ok")
                if i == 3:
                    need("w1t_pe", 8)
                    for b in range(4):
                        copy(UC[0:NCH, :, 2 * b:2 * b + 2, :].rearrange("p g j h -> p j g h"), PS[0:NCH, b, :].rearrange("p (j g h) -> p j g h", j=2, g=SG))
                    tell("uc_ok")
            need("mz_pe")
            copy(MZ[0:2 * SH, :, :].rearrange("p (b g) j -> p b (g j)", b=4), PS[0:2 * SH, 0:4, :])
            tell("mz_ok")
            need("inc_pe")
            for r in range(2):
                for c0 in (0, CCH):
                    dst = ZS[SS:P, r, :, c0:c0 + CCH]
                    src = PS[SS:P, 2 * r:2 * r + 2, :].rearrange("p b (g c) -> p (b g) c", c=NCH)
                    src = src[:, :, c0 + CCH - 1::-1] if c0 == 0 else src[:, :, NCH - 1:CCH - 1:-1]
                    copy(dst, src)
            tell("zs_ok")
            modulation_row(1, 4)
            modulation_row(2, 6)
            need("qss")
            do(act.activation(QST[:, 0:24], QST[:, 24:48], ACT.Sqrt))
            tell("qrs")
            need("qt_pe")
            need("tz_ld", 16 * 15)
            copy(QT[:, :, :].rearrange("p (b i) t -> p b (i t)", b=2), PS[:, 4:6, :])
            tell("qt_ok")

            def probs_turned(n):
                need("pt_pe", n + 1)
                if n:
                    need("pv_pe", n)
                copy(PT[:, :, :].rearrange("p (b c) q -> p b (c q)", b=2), PS[:, 4:6, :])
                tell("pt_ok")
                need("pv_pe", n + 1)
                copy(YAT[:, n % NP, (n // NP) * P:(n // NP + 1) * P], PS[:, 6 + n % 2, 0:P])
                tell("yat_ok")

            for n_ in range(2 * NP):
                need("smax", n_ + 1)
                i = n_ % 2
                for g in range(2):
                    do(act.activation(PR[:, i, g, :], PR[:, i, g, :], ACT.Exp, bias=AC[:, i, 2 + g:3 + g], accum_out=AC[:, i, 6 + g:7 + g]))
                do(act.activation(AC[:, i, 4:6], AC[:, i, 8:10], ACT.Exp))
                tell("sexp")
                if n_:
                    probs_turned(n_ - 1)
            probs_turned(2 * NP - 1)
            need("y_pe")
            for b in range(4):
                copy(YC[0:CCH, :, b * 64:(b + 1) * 64].rearrange("p j (g h) -> p g j h", g=4), PS[0:CCH, b, :].rearrange("p (g j h) -> p g j h", g=4, j=L))
            tell("yc_ok")
            need("gelu_in")
            do(act.activation(YG[:, :], YT1[:, :], ACT.Sigmoid, scale=GELU_S))
            tell("gelu_sg")
            need("glu_pe")
            do(act.activation(YG[:, :], PS[:, 5, :], ACT.Sigmoid))
            tell("glu_ok")
            for m in range(KC):
                b = 4 * (m % 2)
                need("g_pe", 2 * m + 1)
                if m >= 2:
                    need("merg_ok", m - 1)
                do(act.activation(GSG[:, m % 2, 0:2, :], PS[:, b, :].rearrange("p (s t) -> p s t", s=2), ACT.Sigmoid))
                do(act.activation(GSG[:, m % 2, 2, :], PS[:, b + 1, 0:T], ACT.Sigmoid))
                tell("g_sg")
            for row, dst in enumerate((G1ROW, A2ROW, S2ROW, G2ROW)):
                need("row_pe", (row + 1) * KC)
                b = 4 + 2 * (row % 2)
                copy(dst[:, :].rearrange("p (b n) -> p b n", b=2), PS[:, b:b + 2, :])
                tell("row_ok")
            for t in range(TT):
                need("x1_ok", t + 1)
                do(act.activation(H2[:, t, :], X[:, t, :], ACT.Square, accum_out=STAT[:, t:t + 1]))
            tell("ss2")
            need("ss2_ok")
            do(act.activation(STAT[:, 8:10], STAT[:, 4:6], ACT.Sqrt))
            tell("sd2")
            need("h2t_pe")
            copy(H2T[:, :, :].rearrange("p (b k) t -> p b (k t)", b=4), PS[:, 0:4, :])
            tell("h2t_ok")
            need("ex_in")
            for t in range(TT):
                do(act.activation(E4[:, t, 0:4], V8[:, t, 0:4], ACT.Exp, bias=NV0[:, t:t + 1], accum_out=ESUM[:, t:t + 1]))
            tell("ex_out")
            need("qs_ok")
            with act.Fori(0, NE // 2) as pair:
                for par in range(2):
                    e = pair * 2 + par
                    first = act.value_load(qs_t[0:1, bass.ds(e, 1)], min_val=0, max_val=4 * NE)
                    end = act.value_load(qs_t[0:1, bass.ds(e + 1, 1)], min_val=1, max_val=4 * NE)
                    with act.Fori(first, end) as q:
                        act.wait_ge(S["gathered"], q + 1)
                        act.activation(GS, PS[:, 6, :], ACT.Copy).then_inc(S["gs"], 1)
                        act.wait_ge(S["selgt"], q + 2)
                        act.activation(selgt_t[:, :], PS[:, 5, :], ACT.Copy).then_inc(S["xg"], 1)
                        for j in range(2):
                            s = slice(j * T, (j + 1) * T)
                            act.wait_ge(S["glu"], 2 * q + j + 1)
                            act.activation(ACTA[:, s], GL[:, s], ACT.Sigmoid, scale=ALPHA).then_inc(S["sg"], 1)
                            act.wait_ge(S["atp"], 2 * q + j + 1)
                            act.activation(act_t[:, s], PS[:, 7 if j == 0 else 4, 0:T], ACT.Copy).then_inc(S["at"], 1)
                        act.wait_ge(S["dnp"], q + 1)
                        act.activation(GS, PS[:, 6, :], ACT.Copy).then_inc(S["yc"], 1)

        @block.gpsimd
        def _(pool):
            n = [0]

            def do(ins):
                n[0] += 1
                return ins.then_inc(S["pool"], 1)

            def settle():
                pool.wait_ge(S["pool"], n[0])

            def tell(name, k=1):
                settle()
                pool.sem_inc(S[name], k)

            def need(name, k=1):
                pool.wait_ge(S[name], k)

            def load(dst, src, name):
                pool.dma_start(dst, src).then_inc(S[name], 16)

            load(IDN, ident, "const")
            load(BEF, before, "const")
            load(IOTA, iota, "const")
            for at, v, rows in ((V_BMOD, b_mod, 48), (V_N1, norm1_g, KC), (V_N2, norm2_g, KC), (V_C, c, KC), (V_D, ssm_d, 2)):
                load(VROWS[at:at + rows, :], v.rearrange("a (k p) -> (a k) p", p=P), "vec_ld")
            load(VROWS[V_CCTX:V_CCTX + KC, :], c_ctx.rearrange("(k p) -> k p", p=P), "vec_ld")
            load(VROWS[V_TAPS:V_TAPS + 6, :], conv_w[0].rearrange("w (k p) -> (w k) p", p=P), "vec_ld")
            for r, v in enumerate((ssm_c_re, ssm_c_im)):
                for a in range(2):
                    for z in range(2):
                        load(CRAW[:, r, a, z * SS:(z + 1) * SS], v[0, z, a * 8:(a + 1) * 8].rearrange("g h s -> (g h) s"), "c_ld")
            for r, v in enumerate((ssm_b_re, ssm_b_im)):
                for z in range(2):
                    load(BRAW[z * SS:(z + 1) * SS, r, :, :], v[0, z].rearrange("g s h -> s g h"), "braw_ld")
            do(pool.memset(TZ, 0.0))
            settle()
            need("mz_ok")
            for i in range(L):
                load(TZ[i * SH:(i + 1) * SH, :, i * SH:P], MZ[0:SH, :, 0:P - i * SH], "tz_ld")
            for i in range(1, L):
                load(TZ[i * SH:(i + 1) * SH, :, 0:i * SH], MZ[SH:2 * SH, :, (L - 1 - i) * SH:(L - 1) * SH], "tz_ld")
            need("zs_ok", 2)
            need("u2_ok")
            T1, T2 = SCT

            def grow(dst, src, k, shape):
                free = [P] + shape
                n_ = int(np.prod(shape))
                names = " ".join("abc"[:len(shape)])
                t1, t2 = (t[:, 0:n_].rearrange(f"p ({names}) -> p {names}", **dict(zip("abc", shape))) for t in (T1, T2))
                do(pool.tensor_tensor(t1, PAR[:, k, :, :].unsqueeze(3).to_broadcast(free), src, ALU.mult))
                do(pool.tensor_tensor(t2, PAI[:, k, :, :].unsqueeze(3).to_broadcast(free), src[:, ::-1], ALU.mult))
                settle()
                do(pool.tensor_tensor(dst, dst, t1, ALU.add))
                settle()
                do(pool.tensor_tensor(dst, dst, t2, ALU.add))
                settle()

            for lev in range(5):
                st = 2 ** (lev + 1)
                cnt = CCH // st
                grow(ZS[:, :, :, st - 1:CCH:st], ZS[:, :, :, st // 2 - 1:CCH:st], lev, [2, SG, cnt])
            for i in range(1, 8):
                grow(ZS[:, :, :, CCH + i:NCH:8], ZS[:, :, :, CCH + i - 1:NCH:8], 0, [2, SG, 4])
            carry = [31, 3, 7, 11]
            for s_ in range(3):
                do(pool.tensor_copy(ZS[:, :, :, carry[s_ + 1]:carry[s_ + 1] + 1], ZS[:, :, :, CCH + 8 * s_ + 7:CCH + 8 * s_ + 8]))
                settle()
                grow(ZS[:, :, :, carry[s_ + 1]:carry[s_ + 1] + 1], ZS[:, :, :, carry[s_]:carry[s_] + 1], 3, [2, SG, 1])
            for s_ in range(4):
                base = CCH + 8 * s_
                C = ZS[:, :, :, carry[s_]:carry[s_] + 1]
                for r in range(2):
                    shape = [P, SG, 7]
                    zc = C[:, r].to_broadcast(shape)
                    zo = C[:, 1 - r].to_broadcast(shape)
                    t1 = T1[:, r * 128:r * 128 + 112].rearrange("p (g i) -> p g i", g=SG)
                    t2 = T2[:, r * 128:r * 128 + 112].rearrange("p (g i) -> p g i", g=SG)
                    do(pool.tensor_tensor(t1, PA[:, 0, 0:7, :].rearrange("p k g -> p g k"), zc, ALU.mult))
                    do(pool.tensor_tensor(t2, PA[:, 1, 0:7, :].rearrange("p k g -> p g k"), zo, ALU.mult))
                    settle()
                    w = ZS[:, r, :, base:base + 7]
                    do(pool.tensor_tensor(t1, t1, t2, ALU.subtract if r == 0 else ALU.add))
                    settle()
                    do(pool.tensor_tensor(w, w, t1, ALU.add))
            tell("scan_ok")

        @block.vector
        def _(ve):
            n = [0]

            def do(ins):
                n[0] += 1
                return ins.then_inc(S["dve"], 1)

            def settle():
                ve.wait_ge(S["dve"], n[0])

            def tell(name, k=1):
                settle()
                ve.sem_inc(S[name], k)

            def need(name, k=1):
                ve.wait_ge(S[name], k)

            def tt(dst, a, b, op):
                return do(ve.tensor_tensor(dst, a, b, op))

            def ts(dst, a, s1, s2, op0, op1=ALU.bypass):
                return do(ve.tensor_scalar(dst, a, s1, s2, op0) if op1 == ALU.bypass else ve.tensor_scalar(dst, a, s1, s2, op0, op1))

            def stt(dst, a, sc, b, op0, op1):
                return do(ve.scalar_tensor_tensor(out=dst, in0=a, scalar=sc, in1=b, op0=op0, op1=op1))

            def copy(dst, src):
                return do(ve.tensor_copy(dst, src))

            do(ve.memset(ONES, 1.0))
            do(ve.memset(silu_t[:, :], 0.0))
            tell("ones")
            need("vec_t")
            copy(VEC[:, :], PS[:, 7, 0:V_ROWS])
            tell("vec_ok")
            need("silu_ok")
            tt(SILU[:, :, 0:2], VEC[:, V_C:V_C + 16].rearrange("p (v k) -> p k v", v=2), SIG16.rearrange("p (v k) -> p k v", v=2), ALU.mult)
            tell("silu2")
            need("sq_sum")
            ts(STAT[:, 4:8], STAT[:, 0:4], 1.0 / D, EPS, ALU.mult, ALU.add)
            tell("sd_ok")
            need("stat_ok")
            do(ve.reciprocal(STAT[:, 12:16], STAT[:, 8:12]))
            settle()
            for i, src in enumerate((CX[:, 0, :], CX[:, 1, :], X[:, 0, :], X[:, 1, :])):
                ts(XN[:, i, :], src, STAT[:, 12 + i:13 + i], None, ALU.mult)
            tell("xn_ok", 4)
            need("lam_t")
            copy(LAM[:, 2:4, :], PS[:, 6, 0:2 * SG].rearrange("p (r g) -> p r g", r=2))
            tell("lam_ok")
            need("ct_t")
            copy(CT[:, :, :, :].rearrange("p r g h -> p (r g h)"), PS[:, 5, :])
            tell("ct_ok")

            def modulation_columns(third, bank):
                need("modt_pe", third + 1)
                src = PS[:, bank, :].rearrange("p (c q m) -> p q c m", c=4, q=4)[:, :, :, 0:2]
                dst = MOD[:, 2 * third:2 * third + 2, :, :].rearrange("p w (a c) v -> p (w a) c v", c=4)
                bias = VEC[:, V_BMOD + 16 * third:V_BMOD + 16 * third + 16].rearrange("p (q c) -> p q c", c=4).unsqueeze(3).to_broadcast([P, 4, 4, 2])
                tt(dst, src, bias, ALU.add)
                settle()

            modulation_columns(0, 5)
            stt(A1[:, :, :], MOD[:, 1, :, :], 1.0, VEC[:, V_N1:V_N1 + KC].unsqueeze(2).to_broadcast([P, KC, 2]), ALU.add, ALU.mult)
            tell("mod_ok")
            for k in range(1, KC, 2):
                need("xnt_pe", k + 1)
                ts(HT[:, k, T:2 * T], PS[:, k % 4, T:2 * T], A1[:, k, 0:1], MOD[:, 0, k, 0:1], ALU.mult, ALU.add)
                ts(HT[:, k, 0:T], PS[:, k % 4, 0:T], A1[:, k, 1:2], MOD[:, 0, k, 1:2], ALU.mult, ALU.add)
                tell("ht_ok_v")

            L_ = [LAM[:, i, :] for i in range(20)]
            lre, lim, xr, yi, m, t, kk, sn, cm, t2, nr, ni, ar, ai, den, br_, bi_ = L_[2:19]
            dt = L_[1]
            need("dt_ok")
            tt(xr, lre, dt, ALU.mult)
            tt(yi, lim, dt, ALU.mult)
            settle()
            ts(xr, xr, -104.0, 104.0, ALU.max, ALU.min)
            ts(kk, yi, 1.0 / TWO_PI, ROUND, ALU.mult, ALU.add)
            settle()
            ts(xr, xr, 1.0 / 256, None, ALU.mult)
            ts(kk, kk, -ROUND, None, ALU.add)
            settle()
            ts(m, xr, 1.0 / 7, 1.0, ALU.mult, ALU.add)
            stt(yi, kk, -PI_A, yi, ALU.mult, ALU.add)
            settle()
            for d in (6, 5, 4, 3, 2):
                tt(m, m, xr, ALU.mult)
                if d == 6:
                    stt(yi, kk, -PI_B, yi, ALU.mult, ALU.add)
                if d == 5:
                    stt(yi, kk, -PI_C, yi, ALU.mult, ALU.add)
                if d == 4:
                    ts(yi, yi, 0.25, None, ALU.mult)
                if d == 3:
                    tt(t2, yi, yi, ALU.mult)
                settle()
                ts(m, m, 1.0 / d, 1.0, ALU.mult, ALU.add)
                settle()
            tt(m, m, xr, ALU.mult)
            settle()
            for _ in range(8):
                stt(m, m, 2.0, m, ALU.add, ALU.mult)
                settle()
            ts(sn, t2, -1.0 / 110, 1.0, ALU.mult, ALU.add)
            ts(cm, t2, -1.0 / 132, 1.0, ALU.mult, ALU.add)
            settle()
            for ds, dc in ((72, 90), (42, 56), (20, 30), (6, 12)):
                tt(sn, sn, t2, ALU.mult)
                tt(cm, cm, t2, ALU.mult)
                settle()
                ts(sn, sn, -1.0 / ds, 1.0, ALU.mult, ALU.add)
                ts(cm, cm, -1.0 / dc, 1.0, ALU.mult, ALU.add)
                settle()
            tt(sn, sn, yi, ALU.mult)
            stt(cm, cm, -0.5, t2, ALU.mult, ALU.mult)
            settle()
            for _ in range(2):
                stt(t, cm, 1.0, sn, ALU.add, ALU.mult)
                tt(t2, sn, sn, ALU.mult)
                settle()
                ts(sn, t, 2.0, None, ALU.mult)
                ts(cm, t2, -2.0, None, ALU.mult)
                settle()
            stt(nr, cm, 1.0, m, ALU.add, ALU.mult)
            stt(ni, m, 1.0, sn, ALU.add, ALU.mult)
            settle()
            tt(nr, nr, cm, ALU.add)
            tt(t, lre, lre, ALU.mult)
            tt(t2, lim, lim, ALU.mult)
            settle()
            ts(POW[:, 0, 0, :], nr, 1.0, None, ALU.add)
            copy(POW[:, 1, 0, :], ni)
            tt(den, t, t2, ALU.add)
            tt(br_, nr, lre, ALU.mult)
            tt(ar, ni, lim, ALU.mult)
            settle()
            do(ve.reciprocal(den, den))
            tt(br_, br_, ar, ALU.add)
            tt(bi_, ni, lre, ALU.mult)
            tt(ai, nr, lim, ALU.mult)
            settle()
            tt(bi_, bi_, ai, ALU.subtract)
            tt(br_, br_, den, ALU.mult)
            settle()
            tt(bi_, bi_, den, ALU.mult)
            settle()

            def cmul(dr, di, ar, ai, br, bi, tmp, negate=False):
                t0, t1, t2, t3 = tmp
                tt(t0, ar, br, ALU.mult)
                tt(t1, ai, bi, ALU.mult)
                tt(t2, ar, bi, ALU.mult)
                tt(t3, ai, br, ALU.mult)
                settle()
                tt(dr, t0, t1, ALU.subtract)
                if negate:
                    stt(di, t2, -1.0, t3, ALU.mult, ALU.subtract)
                else:
                    tt(di, t2, t3, ALU.add)
                settle()

            small = [even_w[:, 4096 + 256 * i:4096 + 256 * (i + 1)] for i in range(4)]

            def temps(shape):
                n_ = int(np.prod(shape))
                names = " ".join("abc"[:len(shape)])
                return [s[:, 0:n_].rearrange(f"p ({names}) -> p {names}", **dict(zip("abc", shape))) for s in small]

            def powers(W):
                for have in (1, 2, 4):
                    shape = [have, SG]
                    top = [W[:, r, have - 1:have, :].to_broadcast([P] + shape) for r in range(2)]
                    cmul(W[:, 0, have:2 * have, :], W[:, 1, have:2 * have, :], W[:, 0, 0:have, :], W[:, 1, 0:have, :], top[0], top[1], temps(shape))

            powers(POW)
            do(ve.memset(EXPO[:, 0, :, :], 1.0))
            do(ve.memset(EXPO[:, 1, :, :], 0.0))
            settle()
            copy(EXPO[0:SS, :, 1:L, :], POW[0:SS, :, 0:L - 1, :])
            copy(EXPO[SS:P, :, 0:L - 1, :], POW[SS:P, :, L - 2::-1, :])
            need("braw_ld", 64)
            bsh = [P, SG, SH]
            g16 = lambda v: v.unsqueeze(2).to_broadcast(bsh)
            cmul(BP[:, 0, :, :], BP[:, 1, :, :], g16(br_), g16(bi_), BRAW[:, 0, :, :], BRAW[:, 1, :, :], temps([SG, SH]))
            do(ve.memset(BB, 0.0))
            settle()
            for z in range(2):
                copy(BB[z * SS:(z + 1) * SS, :, :, z, :], BP[z * SS:(z + 1) * SS, :, :, :])
            settle()
            cmul(BP[:, 0, :, :], BP[:, 1, :, :], g16(POW[:, 0, 0, :]), g16(POW[:, 1, 0, :]), BP[:, 0, :, :], BP[:, 1, :, :], temps([SG, SH]))
            b4 = [P, SG, L, SH]
            er, ei = (EXPO[:, r, ::-1, :].rearrange("p j g -> p g j").unsqueeze(3).to_broadcast(b4) for r in range(2))
            pr, pi = (BP[:, r, :, :].unsqueeze(2).to_broadcast(b4) for r in range(2))
            tt(TMP[0], er, pr, ALU.mult)
            tt(TMP[1], ei, pi, ALU.mult)
            tt(W1N[:, 1, :, :, :], er, pi, ALU.mult)
            settle()
            tt(W1N[:, 0, :, :, :], TMP[0], TMP[1], ALU.subtract)
            settle()
            tt(TMP[0], ei, pr, ALU.mult)
            settle()
            tt(W1N[:, 1, :, :, :], W1N[:, 1, :, :, :], TMP[0], ALU.add)
            er, ei = (EXPO[:, r, :, :].rearrange("p j g -> p g j").unsqueeze(3).to_broadcast(b4) for r in range(2))
            cr, ci = (CT[:, r, :, :].unsqueeze(2).to_broadcast(b4) for r in range(2))
            tt(TMP[1], er, cr, ALU.mult)
            settle()
            tt(TMP[0], ei, ci, ALU.mult)
            settle()
            tt(CMV[:, 0, :, :, :], TMP[1], TMP[0], ALU.subtract)
            settle()
            tt(TMP[0], er, ci, ALU.mult)
            tt(TMP[1], ei, cr, ALU.mult)
            settle()
            stt(CMV[:, 1, :, :, :], TMP[0], -1.0, TMP[1], ALU.mult, ALU.subtract)
            settle()
            copy(PA[:, :, 0, :], POW[:, :, L - 1, :])
            settle()
            powers(PA)
            cmul(PAR[:, 4, 0, :], PAI[:, 4, 1, :], PA[:, 0, 7, :], PA[:, 1, 7, :], PA[:, 0, 7, :], PA[:, 1, 7, :], temps([SG]))
            copy(PAR[:, 4, 1, :], PAR[:, 4, 0, :])
            ts(PAI[:, 4, 0, :], PAI[:, 4, 1, :], -1.0, None, ALU.mult)
            for lev in range(4):
                k = 2 ** lev - 1
                for r in range(2):
                    copy(PAR[:, lev, r, :], PA[:, 0, k, :])
                    ts(PAI[:, lev, r, :], PA[:, 1, k, :], -1.0 if r == 0 else 1.0, None, ALU.mult)
            tell("tabs_ok")

            need("bcx_ok", 6)
            z_ = BCX[:, 2:4, :]
            tt(z_, BCX[:, 2:4, :], BCX[:, 4:6, :], ALU.mult)
            settle()
            for m_ in range(2):
                tap = [VEC[:, V_TAPS + 2 * w + m_:V_TAPS + 2 * w + m_ + 1] for w in range(3)]
                o, zz = YCONV[:, m_, :], BCX[:, 2 + m_, :]
                ts(o, zz, tap[1], None, ALU.mult)
                settle()
                stt(o[:, 1:T], zz[:, 0:T - 1], tap[0], o[:, 1:T], ALU.mult, ALU.add)
                settle()
                stt(o[:, 0:T - 1], zz[:, 1:T], tap[2], o[:, 0:T - 1], ALU.mult, ALU.add)
                settle()
            tt(YCONV, YCONV, BCX[:, 0:2, :], ALU.mult)
            tell("yconv_ok")

            need("qk_ld", 80)
            need("kcx_ok", 2)
            need("qk_ok", 4)
            need("mz_pe")
            HH = NQ + NKV
            QF = QK[:, :, :, :].rearrange("p t h d -> p (t h) d")
            SQ = QP[:, :, :, :].rearrange("p t i (g d) -> p (t i g) d", g=2)
            KF = KCX[:, :, :, :].rearrange("p t h d -> p (t h) d")
            tt(SQ, QF, QF, ALU.mult)
            settle()
            do(ve.tensor_reduce(QST[:, 24:44], SQ, AX.X, ALU.add))
            settle()
            tt(SQ[:, 0:4, :], KF, KF, ALU.mult)
            settle()
            do(ve.tensor_reduce(QST[:, 44:48], SQ[:, 0:4, :], AX.X, ALU.add))
            settle()
            ts(QST[:, 24:48], QST[:, 24:48], 1.0 / HD, EPS, ALU.mult, ALU.add)
            tell("qss")
            need("u2_pe")
            copy(U2[:, :, :].rearrange("p (b g) c -> p b (g c)", b=2), PS[:, 4:6, :])
            tell("u2_ok")
            need("inc_pe")
            copy(ZS[0:SS, :, :, :].rearrange("p r (b g) c -> p (r b) (g c)", b=2), PS[0:SS, 0:4, :])
            tell("zs_ok")
            modulation_columns(1, 5)
            modulation_columns(2, 7)
            stt(A2, MOD[:, 4, :, 0], 1.0, VEC[:, V_N2:V_N2 + KC], ALU.add, ALU.mult)
            tell("mod_ok", 2)
            need("qrs")
            do(ve.reciprocal(QST[:, 48:72], QST[:, 0:24]))
            settle()
            tt(QF, QF, QST[:, 48:68].unsqueeze(2).to_broadcast([P, TT * HH, HD]), ALU.mult)
            tt(KF, KF, QST[:, 68:72].unsqueeze(2).to_broadcast([P, TT * NKV, HD]), ALU.mult)
            settle()
            for t_ in range(TT):
                tt(QK[:, t_, 0:NQ, :], QK[:, t_, 0:NQ, :], QKG[:, 0:1, :].to_broadcast([P, NQ, HD]), ALU.mult)
                tt(QK[:, t_, NQ:HH, :], QK[:, t_, NQ:HH, :], QKG[:, 1:2, :].to_broadcast([P, NKV, HD]), ALU.mult)
            tt(KF, KF, QKG[:, 1:2, :].to_broadcast([P, TT * NKV, HD]), ALU.mult)
            settle()
            half = HD // 2
            shape = [P, TT, HH, half]
            co, si = COS.unsqueeze(2).to_broadcast(shape), SIN.unsqueeze(2).to_broadcast(shape)
            QPH = QP[:, :, :, :].rearrange("p t i (g d) -> p t (i g) d", g=2)
            rt1 = PR[:, 0, :, :].rearrange("p h k -> p (h k)")[:, 0:TT * HH * half].rearrange("p (t h d) -> p t h d", t=TT, h=HH)
            rt2 = PR[:, 1, :, :].rearrange("p h k -> p (h k)")[:, 0:TT * HH * half].rearrange("p (t h d) -> p t h d", t=TT, h=HH)
            x1, x2 = QK[:, :, :, 0:half], QK[:, :, :, half:HD]
            need("modt_pe", 3)
            tt(QPH[:, :, :, 0:half], x1, co, ALU.mult)
            tt(rt1, x2, si, ALU.mult)
            tt(QPH[:, :, :, half:HD], x1, si, ALU.mult)
            tt(rt2, x2, co, ALU.mult)
            settle()
            tt(QPH[:, :, :, 0:half], QPH[:, :, :, 0:half], rt1, ALU.subtract)
            tt(QPH[:, :, :, half:HD], QPH[:, :, :, half:HD], rt2, ALU.add)
            tell("qp_ok")
            need("tz_ld", 16 * 15)
            do(ve.memset(KT, 0.0))
            settle()
            need("qt_pe")
            for g in range(NKV):
                copy(KT[g * HD:(g + 1) * HD, g, :], PS[g * HD:(g + 1) * HD, 6, :])
            tell("qt_ok")
            need("mask_ld", 16)
            for k in range(2 * NP):
                t_, i, b = k // NP, k % NP, k % 2
                need("s_pe", k + 1)
                if k >= 2:
                    need("pt_pe", k - 1)
                stt(PR[:, b, :, :], PS[:, 2 * b:2 * b + 2, :], HD ** -0.5, MASK[:, t_:t_ + 1, :].to_broadcast([P, 2, BANK]), ALU.mult, ALU.add)
                tell("s_ok")
                do(ve.tensor_reduce(AC[:, b, 0:2], PR[:, b, :, :], AX.X, ALU.max))
                settle()
                tt(AC[:, b, 0:2], AC[:, b, 0:2], SINKS[:, i::NP], ALU.max)
                settle()
                ts(AC[:, b, 2:4], AC[:, b, 0:2], -1.0, None, ALU.mult)
                tt(AC[:, b, 8:10], SINKS[:, i::NP], AC[:, b, 0:2], ALU.subtract)
                tell("smax")
                need("sexp", k + 1)
                tt(AC[:, b, 10:12], AC[:, b, 6:8], AC[:, b, 4:6], ALU.add)
                settle()
                do(ve.reciprocal(AC[:, b, 10:12], AC[:, b, 10:12]))
                settle()
                for g in range(2):
                    ts(PR[:, b, g, :], PR[:, b, g, :], AC[:, b, 10 + g:11 + g], None, ALU.mult)
                tell("p_ok")
            need("scan_ok")
            carry = [31, 3, 7, 11]
            for z in range(2):
                h = slice(z * SS, (z + 1) * SS)
                for s_ in range(4):
                    at = s_ * 8
                    if z == 0:
                        first, rest = ZR[h, :, :, at:at + 1], ZR[h, :, :, at + 1:at + 8]
                    else:
                        first = ZR[h, :, :, CCH - 1 - at:CCH - at]
                        lo = CCH - 8 - at
                        rest = ZR[h, :, :, lo:lo + 7][:, :, :, ::-1]
                    copy(first, ZS[h, :, :, carry[s_]:carry[s_] + 1])
                    copy(rest, ZS[h, :, :, CCH + at:CCH + at + 7])
            tell("zr_ok")
            need("yt_pe")
            for m_ in range(2):
                stt(YS[:, m_, :].rearrange("p (c j) -> p c j", j=L), UT[:, m_, T:2 * T].rearrange("p (c j) -> p c j", j=L), VEC[:, V_D + m_:V_D + m_ + 1],
                    PS[:, 4, m_ * T:(m_ + 1) * T].rearrange("p (j c) -> p c j", j=L), ALU.mult, ALU.add)
            settle()
            yf = YS[:, :, :].rearrange("p m t -> p (m t)")
            tt(YT1, yf, yf, ALU.mult)
            settle()
            ts(YT1, YT1, GELU_C, 1.0, ALU.mult, ALU.add)
            settle()
            tt(YT1, YT1, yf, ALU.mult)
            tell("gelu_in")
            need("gelu_sg")
            tt(yf, yf, YG, ALU.mult)
            tell("z_ok")
            need("glu_ok")
            tt(YA[:, :, :].rearrange("p m t -> p (m t)"), yf, YG, ALU.mult)
            tell("yssm_ok")
            for m_ in range(KC):
                b = 4 * (m_ % 2)
                need("g_sg", m_ + 1)
                need("g_pe", 2 * m_ + 2)
                g_ = GSG[:, m_ % 2, :, :]
                tt(g_[:, 0:2, :], g_[:, 0:2, :], PS[:, b + 2, :].rearrange("p (s t) -> p s t", s=2), ALU.mult)
                tt(g_[:, 2, :], g_[:, 2, :], PS[:, b + 3, 0:T], ALU.mult)
                settle()
                tt(g_[:, 0, :], g_[:, 0, :], g_[:, 1, :], ALU.add)
                settle()
                tt(MERG[:, m_, :], g_[:, 0, :], g_[:, 2, :], ALU.add)
                tell("merg_ok")
            ve.sem_inc(S["merge_done"], 1)
            cols = [MOD[:, 2, :, 0], A2, MOD[:, 3, :, 0], MOD[:, 5, :, 0]]
            need("g_pe", 16)
            for row in range(4):
                for k in range(KC):
                    at = row * KC + k
                    if at >= 4:
                        need("row_pe", at - 3)
                    ts(DG[:, at % 4, :], IDN, cols[row][:, k:k + 1], None, ALU.mult)
                    tell("dgk")
            need("row_ok", 4)
            need("wo_pe")
            for t_ in range(TT):
                mix = H2[:, t_, :]
                tt(mix.rearrange("p (b n) -> p b n", b=2), PS[:, 2 * t_:2 * t_ + 2, :], G1ROW[:, :].rearrange("p (b n) -> p b n", b=2), ALU.mult)
                settle()
                tt(X[:, t_, :], X[:, t_, :], mix, ALU.add)
                tell("x1_ok")
            need("ss2")
            ts(STAT[:, 4:6], STAT[:, 0:2], 1.0 / D, EPS, ALU.mult, ALU.add)
            tell("ss2_ok")
            need("sd2")
            do(ve.reciprocal(STAT[:, 12:14], STAT[:, 8:10]))
            settle()
            for t_ in range(TT):
                stt(H2[:, t_, :], X[:, t_, :], STAT[:, 12 + t_:13 + t_], A2ROW, ALU.mult, ALU.mult)
                settle()
                tt(H2[:, t_, :], H2[:, t_, :], S2ROW, ALU.add)
                tell("h2_ok")
            need("rt_pe")
            do(ve.memset(silu_t[:, :], 0.0))
            for t_ in range(TT):
                copy(LG[:, t_, :], PS[:, 6, t_ * 64:t_ * 64 + NE])
            settle()
            for t_ in range(TT):
                do(ve.max(V8[:, t_, :], LG[:, t_, :]))
            settle()
            for t_ in range(TT):
                do(ve.max_index(I8[:, t_, :], V8[:, t_, :], LG[:, t_, :]))
                ts(NV0[:, t_:t_ + 1], V8[:, t_, 0:1], -1.0, None, ALU.mult)
            tell("ex_in")
            copy(I8F[:, :, :], I8[:, :, :])
            need("ex_out")
            do(ve.reciprocal(ERCP[:, 0:2], ESUM[:, 0:2]))
            settle()
            tt(G4[:, :, 0:4], E4[:, :, 0:4], ERCP[:, 0:2].unsqueeze(2).to_broadcast([P, TT, 4]), ALU.mult)
            settle()
            for k in range(4):
                for t_ in range(TT):
                    ts(TE[:, t_, :], IOTA[:, 0:NE], I8F[:, t_, k:k + 1], G4[:, t_, k:k + 1], ALU.is_equal, ALU.mult)
                    ts(PM[:, t_, :], IOTA[:, 0:NE], I8F[:, t_, k:k + 1], None, ALU.is_equal)
                settle()
                if k == 0:
                    copy(GM, TE)
                    copy(MK, PM)
                else:
                    tt(GM, GM, TE, ALU.add)
                    tt(MK, MK, PM, ALU.add)
                settle()
            tell("mk_ok")
            need("pos_pe")
            copy(CNT[0:NE, :], PS[0:NE, 7, 128:129])
            copy(GT[0:NE, 0:T], PS[0:NE, 7, 256:512])
            settle()
            ts(NBK[0:NE, :], CNT[0:NE, :], float(NB), 1.0, ALU.is_gt, ALU.add)
            settle()
            for k in (2, 3):
                ts(C1[0:NE, :], CNT[0:NE, :], float(k * NB), None, ALU.is_gt)
                settle()
                tt(NBK[0:NE, :], NBK[0:NE, :], C1[0:NE, :], ALU.add)
                settle()
            tell("tab")
            for t_ in range(TT):
                stt(PM[:, t_, :], PS[:, 7, t_ * 64:t_ * 64 + NE], 1.0, MK[:, t_, :], ALU.add, ALU.mult)
            settle()
            ts(PM, PM, -1.0, None, ALU.add)
            need("qs_pe")
            copy(qs_t[:, :], PS[0:1, 6, 0:NE + 1])
            need("acc0")
            tell("qs_ok")
            ve.sem_inc(S["shift"], 1)
            ve.sem_inc(S["selgt"], 1)
            with ve.Fori(0, NE // 2) as pair:
                for par in range(2):
                    e = pair * 2 + par
                    first = ve.value_load(qs_t[0:1, bass.ds(e, 1)], min_val=0, max_val=4 * NE)
                    end = ve.value_load(qs_t[0:1, bass.ds(e + 1, 1)], min_val=1, max_val=4 * NE)
                    with ve.Fori(first, end) as q:
                        ve.wait_ge(S["shift"], q + 1)
                        ve.wait_ge(S["selgt"], q + 1)
                        for t in range(TT):
                            ve.tensor_scalar(SEL[:, t, :], IOTA[:, 0:NB], PM[:, t, bass.ds(e, 1)], None, ALU.is_equal)
                            last = ve.tensor_scalar(SELG[:, t, NB:2 * NB], IOTA[:, 0:NB], PM[:, t, bass.ds(e, 1)], GM[:, t, bass.ds(e, 1)], ALU.is_equal, ALU.mult)
                        last.then_inc(S["sel"], 1)
                        ve.wait_ge(S["sel"], q + 1)
                        ve.tensor_scalar(PM[:, :, bass.ds(e, 1)], PM[:, :, bass.ds(e, 1)], float(-NB), None, ALU.add).then_inc(S["shift"], 1)
                        ve.wait_ge(S["xt"], q + 1)
                        ve.tensor_copy(XG[:, :, :], PS[:, 7, :]).then_inc(S["xg"], 1)
                        for j in range(2):
                            s = slice(T * j, T * (j + 1))
                            ve.wait_ge(S["gup"], 2 * q + j + 1)
                            ve.tensor_scalar(GL[:, s], PS[:, 4 + j, 0::2], LIMIT, None, ALU.min).then_inc(S["glu"], 1)
                            ve.tensor_scalar(UP[:, s], PS[:, 4 + j, 1::2], LIMIT, -LIMIT, ALU.min, ALU.max).then_inc(S["actm"], 1)
                            ve.wait_ge(S["glu"], 2 * q + j + 1)
                            ve.wait_ge(S["actm"], 4 * q + 2 * j + 1)
                            ve.scalar_tensor_tensor(out=UP[:, s], in0=UP[:, s], scalar=1.0, in1=GL[:, s], op0=ALU.add, op1=ALU.mult).then_inc(S["actm"], 1)
                            ve.wait_ge(S["actm"], 4 * q + 2 * j + 2)
                            ve.wait_ge(S["sg"], 2 * q + j + 1)
                            ve.tensor_tensor(ACTA[:, s], UP[:, s], ACTA[:, s], ALU.mult).then_inc(S["act"], 1)
            blocks = ve.value_load(qs_t[0:1, NE:NE + 1], min_val=1, max_val=4 * NE)
            ve.wait_ge(S["scat"], blocks)
            for t_ in range(TT):
                ve.tensor_tensor(H2[:, t_, :].rearrange("p (b n) -> p b n", b=2), PS[:, 2 * t_:2 * t_ + 2, :], G2ROW[:, :].rearrange("p (b n) -> p b n", b=2), ALU.mult).then_inc(S["dgk"], 1)
            ve.wait_ge(S["dgk"], 4 * KC + TT)
            ve.tensor_tensor(X, X, H2, ALU.add).then_inc(S["fin"], 1)


def tables():
    tok = np.arange(T)
    n_pairs = HD // 4
    inv = (10000.0 ** (-np.arange(n_pairs, dtype=np.float32) / n_pairs)).astype(np.float32)
    ang = np.concatenate([(tok // GRID_W).astype(np.float32)[:, None] * inv, (tok % GRID_W).astype(np.float32)[:, None] * inv], axis=-1)
    far = np.abs(tok[:, None] - tok[None, :]) > 128
    return {
        "ident": np.eye(P, dtype=np.float32),
        "before": np.triu(np.ones((P, P), np.float32), 1),
        "iota": np.tile(np.arange(NB, dtype=np.float32), (P, 1)),
        "cosine": np.cos(ang).astype(np.float32),
        "sine": np.sin(ang).astype(np.float32),
        "window": np.concatenate([np.zeros((T, T)), np.where(far, NEG, 0.0)], axis=1).astype(np.float32),
    }


NAMES = """x c ctx c_ctx w_mod b_mod norm1_g norm2_g w_in ssm_lam_re ssm_lam_im ssm_log_dt ssm_b_re ssm_b_im
    ssm_c_re ssm_c_im ssm_d w_glu w_ssm_out conv_w w_conv_out q_norm_g k_norm_g attn_sinks w_attn_out w_o
    w_router b_router w_gate_up b_gate_up w_down b_down""".split()


def kernel(**inputs):
    from concourse import bacc
    from concourse.bass_utils import run_bass_kernel_spmd

    nc = bacc.Bacc("TRN2", target_bir_lowering=False, num_devices=1)
    arrays = {n: np.ascontiguousarray(inputs[n]) for n in NAMES}
    arrays.update(tables())
    args = {n: nc.dram_tensor(f"in_{n}", a.shape, mybir.dt.from_np(a.dtype), kind="ExternalInput").ap() for n, a in arrays.items()}
    out = nc.dram_tensor("out", (1, T, D), F32, kind="ExternalOutput").ap()
    build(nc, out=out, **args)
    r = run_bass_kernel_spmd(nc, [{f"in_{n}": a for n, a in arrays.items()}], core_ids=[0])
    return r.results[0]["out"]
```

```python
from contextlib import ExitStack
import math

import numpy as np

import concourse.bass as bass
from concourse import mybir

ALU = mybir.AluOpType
ACT = mybir.ActivationFunctionType
AX = mybir.AxisListType
F32 = mybir.dt.float32
I32 = mybir.dt.int32
U32 = mybir.dt.uint32

P = 128
D = 1024
KC = D // P
T = 256
TT = T // P
GRID_W = 64
HD, NQ, NKV = 64, 8, 2
NP = NQ // NKV
SG, SH, SS = 16, 16, 64
L = 8
NCH = 2 * T // L
CCH = NCH // 2
NE, F = 32, 1024
FC = F // P
NB = 64
EPS = 1e-6
LIMIT, ALPHA = 7.0, 1.702
NEG = -1e30
BANK = 512
TWO_PI = 2 * math.pi
PI_A = 6.28125
PI_B = float(np.float32(np.floor((TWO_PI - PI_A) * 2**20) / 2**20))
PI_C = float(np.float32(TWO_PI - PI_A - PI_B))
ROUND = 1.5 * 2**23
GELU_C, GELU_S = 0.044715, 2 * math.sqrt(2 / math.pi)

V_BMOD, V_N1, V_N2, V_C, V_CCTX, V_D, V_TAPS, V_ROWS = 0, 48, 56, 64, 72, 80, 82, 88


def build(nc, x, c, ctx, c_ctx, w_mod, b_mod, norm1_g, norm2_g, w_in, ssm_lam_re, ssm_lam_im,
          ssm_log_dt, ssm_b_re, ssm_b_im, ssm_c_re, ssm_c_im, ssm_d, w_glu, w_ssm_out, conv_w,
          w_conv_out, q_norm_g, k_norm_g, attn_sinks, w_attn_out, w_o, w_router, b_router,
          w_gate_up, b_gate_up, w_down, b_down, ident, before, iota, cosine, sine, window, out):
    with ExitStack() as stack:
        def sbuf(name, width, dtype=F32):
            return stack.enter_context(nc.sbuf_tensor(name, [P, width], dtype))

        even_w = sbuf("even_w", KC * 2 * F)
        odd_w = sbuf("odd_w", KC * 2 * F)
        down_w = sbuf("down_w", FC * D)
        toks = sbuf("toks", TT * D)
        hid = sbuf("hid", TT * D)
        wide = sbuf("wide", 4096)
        idn_t = sbuf("idn", P)
        bef_t = sbuf("bef", P)
        iota_t = sbuf("iota", NB)
        ones_t = sbuf("ones", P)
        silu_t = sbuf("silu", 3 * P)
        selgt_t = sbuf("selgt", 2 * T)
        act_a = sbuf("act_a", 512)
        act_t = sbuf("act_t", 512)
        ut_t = sbuf("ut", 1024)
        vec_t = sbuf("vec", V_ROWS)
        mod_t = sbuf("mod", 96)
        ab_t = sbuf("ab", 24)
        rt_t = sbuf("rt", 400)
        rt_i = sbuf("rt_i", 16, U32)
        qs_t = stack.enter_context(nc.sbuf_tensor("qs", [1, NE + 1], I32))

        def view(t, at, pattern, /, **sizes):
            n = 1
            for v in sizes.values():
                n *= v
            names = list(sizes)
            return t[:, at:at + n].rearrange(f"p ({' '.join(names)}) -> p {pattern or ' '.join(names)}", **sizes)

        GU = [view(even_w, 0, "", k=KC, n=2 * F), view(odd_w, 0, "", k=KC, n=2 * F)]
        DN = view(down_w, 0, "", k=FC, n=D)
        X = view(toks, 0, "", t=TT, d=D)
        H2 = view(hid, 0, "", t=TT, d=D)
        CX = H2
        ZS = view(hid, 0, "", r=2, g=SG, c=NCH)
        ZR = view(even_w, 15360, "", r=2, g=SG, c=CCH)
        SCT = [even_w[:, 1024:1536], even_w[:, 1536:2048]]
        HT = view(wide, 0, "", k=KC, t=2 * T)
        H2T = view(wide, 0, "", k=KC, t=T)
        BROW = wide[:, 2048:4096]
        XG, GL, UP, XS = view(wide, 0, "", c=4, n=P), wide[:, 512:1024], wide[:, 1024:1536], wide[:, 1536:2048]
        SELGT = view(selgt_t, 0, "", h=2, t=T)
        IDN, BEF, IOTA, ONES = idn_t[:, :], bef_t[:, :], iota_t[:, :], ones_t[:, :]
        SILU = view(silu_t, 0, "", k=KC, m=32)
        SELG = view(silu_t, 0, "", t=TT, n=NB)
        COS, SIN = view(act_a, 320, "", t=TT, d=32), view(act_a, 384, "", t=TT, d=32)
        SEL = view(rt_t, 0, "", t=TT, n=NB)
        ACTA, ACTT = act_a, view(act_t, 0, "", c=4, n=P)
        YS_E = act_a[:, :]
        UT = view(ut_t, 0, "", m=2, t=2 * T)
        G2ROW = ut_t
        VEC = vec_t
        MOD = view(mod_t, 0, "", w=6, k=KC, v=2)
        A1 = view(ab_t, 0, "", k=KC, v=2)

        LG, MK, GM, TE = (view(rt_t, 64 * i, "", t=TT, e=NE) for i in range(4))
        PM = view(rt_t, 256, "", t=TT, e=NE)
        V8, I8F, E4, G4 = (view(rt_t, 320 + 16 * i, "", t=TT, n=8) for i in range(4))
        NV0, ESUM, ERCP, CNT, NBK, C1 = (rt_t[:, 384 + 2 * i:386 + 2 * i] for i in range(6))
        NBK, CNT, C1 = NBK[:, 0:1], CNT[:, 0:1], C1[:, 0:1]
        I8 = view(rt_i, 0, "", t=TT, n=8)
        STAT = rt_t[:, 320:384]
        PAR, PAI = (view(down_w, 7808 + 160 * i, "", k=5, r=2, g=SG) for i in range(2))
        PA = view(selgt_t, 256, "", r=2, k=8, g=SG)
        QST = rt_t[:, 64:136]
        AC = view(rt_t, 160, "", b=2, n=12)
        SINKS = act_a[:, 448:456]
        SIG16 = act_a[:, 496:512]
        YT1, YG = down_w[:, 6656:7168], down_w[:, 7168:7680]
        W1N = view(even_w, 0, "", r=2, g=SG, j=L, h=SH)
        MZ = view(down_w, 2048, "", g=SG, j=P)
        UC = view(even_w, 0, "", g=SG, j=L, h=SH)
        YC = view(hid, 0, "", j=L, d=T)
        U2 = view(even_w, 2048, "", g=SG, c=NCH)
        YS, YA = view(down_w, 1024, "", m=2, t=T), view(down_w, 1536, "", m=2, t=T)
        W1T = view(even_w, 4096, "", r=2, g=SG, s=P)
        TMP = [view(even_w, 4096 + 2048 * i, "", g=SG, j=L, h=SH) for i in range(2)]
        CM = view(even_w, 8192, "", r=2, g=SG, j=P)
        CMV = view(even_w, 8192, "", r=2, g=SG, j=L, h=SH)
        TZ = view(even_w, 12288, "", g=SG, j=P)
        QP = view(even_w, 14336, "", t=TT, i=NP + 1, d=P)
        BB = view(even_w, 14336, "", r=2, g=SG, z=2, h=SH)
        BP = view(even_w, 14336 + 1024, "", r=2, g=SG, h=SH)
        YCONV = view(act_t, 0, "", m=2, t=T)
        CT = view(hid, 0, "", r=2, g=SG, h=SH)
        BRAW = view(down_w, 5632, "", r=2, g=SG, h=SH)
        CRAW = view(down_w, 6144, "", r=2, a=2, s=P)
        LRAW = rt_t[0:SG, 0:256].rearrange("p (r s) -> p r s", r=2)
        LAM = view(act_a, 0, "", n=20, g=SG)
        POW = view(selgt_t, 0, "", r=2, k=L, g=SG)
        EXPO = view(selgt_t, 256, "", r=2, j=L, g=SG)
        SSMO = view(even_w, 6144, "", k=2, n=D)
        CONVO = view(even_w, 4096, "", k=2, n=D)
        ATTO = view(even_w, 8192, "", k=NP, n=D)
        VROWS = down_w[:, 8064:8192]
        MODR = [act_t[:, :], even_w[:, 3072:3584], down_w[:, 6144:6656]]
        XN = view(down_w, 0, "", t=4, d=D)
        QK = view(down_w, 0, "", t=TT, h=NQ + NKV, d=HD)
        YAT = view(down_w, 0, "", i=NP, t=T)
        KCX = view(down_w, 1280, "", t=TT, h=NKV, d=HD)
        VV = view(down_w, 1536, "", c=4, d=P)
        QT = view(down_w, 2048, "", i=NP, t=T)
        KT = view(down_w, 3072, "", g=2, t=2 * T)
        PR = view(down_w, 4096, "", b=2, h=2, k=BANK)
        BCX = view(down_w, 4096, "", i=6, t=T)
        PT = view(even_w, 0, "", c=4, q=2 * P)
        QKG = view(down_w, 7680, "", q=2, d=HD)
        MASK = view(down_w, 6656, "", t=TT, k=BANK)
        N2ROW = down_w[:, 2048:3072]
        WR = view(down_w, 7680, "", k=KC, e=NE)
        BR = down_w[:, 7936:7968]
        
        G1ROW, A2ROW, S2ROW = down_w[:, 3072:4096], down_w[:, 4096:5120], down_w[:, 5120:6144]
        WGLU = view(odd_w, 9216, "", k=2, n=T)
        SG_ = view(odd_w, 10240, "", m=KC, s=3, t=T)
        MERG = SG_[:, :, 0, :]
        RG = [view(odd_w, 3072 * i, "", k=KC, s=3, n=P) for i in range(3)]

        names = (
            "dn_ld0 dn_ld1 wm2_ld wu_ld vec2_ld x_ld const c_ld lam_ld braw_ld qk_ld ra_ld rb_ld wglu_ld "
            "br_ld router_ld mask_ld bd_ld vec_ld tz_ld idn_ld bias_ld g_ld0 g_ld1 g_ld2 wo_ld n2_ld "
            "wq0 wq1 wq2 wq3 wq4 wq5 wq6 wq7 "
            "ra_free rb_free wm2_pe "
            "dve act_s pool "
            "gt_pe mod0_pe vec_t modt_pe xnt_pe lam_t ct_t w1t_pe mz_pe u_pe bcx_pe kcx_pe qk_pe u2_pe "
            "inc_pe y_pe yt_pe glu_pe qt_pe s_pe pt_pe pv_pe g_pe wo_pe row_pe br_pe g2_pe h2t_pe rt_pe "
            "pos_pe qs_pe "
            "ys_zero gm_ok gt_ok tz_zero rowsel_ok sq_sum sd_ok sd2 vec_ok silu_ok silu2 modr_ok mod_ok "
            "stat_ok xn_ok ht_ok_a ht_ok_v lam_ok ct_ok dt_ok tabs_ok w1t_ok mz_ok ut_ok bcx_ok kcx_ok qk_ok "
            "yconv_ok uc_ok u2_ok zs_ok scan_ok zr_ok yc_ok gelu_in gelu_sg z_ok glu_ok yssm_ok qss qrs "
            "qp_ok qt_ok s_ok smax sexp p_ok pt_ok yat_ok g_sg merg_ok row_ok a2_ok mod_row x1_ok ss2 ss2_ok "
            "h2_ok h2t_ok ex_in ex_out mk_ok tab qs_ok "
            "shift sel gathered selgt selgtc xs xt xg gup glu sg actm act atp at dnp_half dnp yc scat fin "
            "out_s "
        ).split()
        S = {n: stack.enter_context(nc.semaphore("s_" + n)) for n in names}
        PS = stack.enter_context(nc.psum_tensor("ps", [P, 8, BANK], F32))
        block = stack.enter_context(nc.Block())

        w_mod_v = w_mod[0].rearrange("(k p) n -> p k n", p=P)
        w_in_v = w_in[0].rearrange("(k p) n -> p k n", p=P)
        RA = view(odd_w, 0, "", k=KC, n=1024)
        WM0 = view(even_w, 0, "", k=KC, n=2048)
        WM2 = even_w[:, 6144:8192]
        SQ2 = down_w[:, 1024:2048]
        HIT = view(act_t, 0, "", t=TT, e=NE, k=4)
        ROWSEL = view(even_w, 14336, "", q=4, n=P)
        RAM, RBM = view(odd_w, 0, "", k=4, n=2048), view(odd_w, 8192, "", k=4, n=2048)
        w_gate_v = w_in_v[:, :, 1792:1792 + 3 * D].rearrange("p k (s m n) -> p k s m n", s=3, m=KC)

        @block.sync
        def _(sp):
            def load(dst, src, name):
                sp.dma_start(dst, src).then_inc(S[name], 16)
            load(IDN, ident, "idn_ld")
            for at, v, rows in ((V_C, c, KC), (V_BMOD, b_mod, 48), (V_N1, norm1_g, KC), (V_N2, norm2_g, KC), (V_D, ssm_d, 2)):
                load(VROWS[at:at + rows, :], v.rearrange("a (k p) -> (a k) p", p=P), "vec_ld")
            for k in range(KC):
                load(WM0[:, k, :], w_mod_v[:, k, 0:2048], f"wq{k}")
            load(RA[:, :, 0:T], w_in_v[:, :, 0:T], "wu_ld")
            load(RA[:, :, T:1024], w_in_v[:, :, T:1024], "ra_ld")
            load(view(odd_w, 8192, "", k=KC, n=768), w_in_v[:, :, 1024:1792], "rb_ld")
            sp.wait_ge(S["bcx_pe"], 6)
            for k in range(4):
                load(RAM[:, k, :], w_mod_v[:, k, 2048:4096], "ra_ld")
            sp.wait_ge(S["qk_pe"], TT)
            for k in range(4):
                load(RBM[:, k, :], w_mod_v[:, 4 + k, 2048:4096], "rb_ld")
            sp.wait_ge(S["w1t_pe"], 8)
            for i in (1, 2):
                for q in range(4):
                    at = i * 2048 + q * BANK
                    load(MODR[i][32 * q:32 * q + 32, :], b_mod[0:1, at:at + BANK].to_broadcast([32, BANK]), "bias_ld")
            sp.wait_ge(S["tz_zero"], 1)
            sp.wait_ge(S["mz_ok"], 1)
            for i in range(L):
                load(TZ[i * SH:(i + 1) * SH, :, i * SH:P], MZ[0:SH, :, 0:P - i * SH], "tz_ld")
            for i in range(1, L):
                load(TZ[i * SH:(i + 1) * SH, :, 0:i * SH], MZ[SH:2 * SH, :, (L - 1 - i) * SH:(L - 1) * SH], "tz_ld")
            for m in range(KC):
                if m == 0:
                    sp.wait_ge(S["ra_free"], 1)
                if m == 2:
                    sp.wait_ge(S["rb_free"], 1)
                    load(WGLU, w_glu[0].rearrange("(k p) n -> p k n", p=P), "wglu_ld")
                if m >= 3:
                    sp.wait_ge(S["g_pe"], m - 2)
                for s_ in range(3):
                    load(RG[m % 3][:, :, s_, :], w_gate_v[:, :, s_, m, :], f"g_ld{m % 3}")
                if m == 2:
                    sp.wait_ge(S["inc_pe"], 1)
                    load(WM2, w_mod_v[:, 0, 4096:6144], "wm2_ld")
                    load(CONVO, w_conv_out[0].rearrange("(k p) n -> p k n", p=P), "br_ld")
                if m >= 3:
                    sp.wait_ge(S["wm2_pe"], m - 2)
                    load(WM2, w_mod_v[:, m - 2, 4096:6144], "wm2_ld")
            for k in (6, 7):
                sp.wait_ge(S["wm2_pe"], k)
                load(WM2, w_mod_v[:, k, 4096:6144], "wm2_ld")
            sp.wait_ge(S["s_pe"], 2 * NP)
            load(N2ROW, norm2_g.to_broadcast([P, D]), "n2_ld")
            sp.wait_ge(S["wm2_pe"], KC)
            load(SSMO, w_ssm_out[0].rearrange("(k p) n -> p k n", p=P), "br_ld")
            sp.wait_ge(S["y_pe"], 4)
            for g in range(NKV):
                load(ATTO[g * HD:(g + 1) * HD], w_attn_out[0, g * NP * HD:(g + 1) * NP * HD].rearrange("(i d) n -> d i n", d=HD), "br_ld")
            sp.wait_ge(S["g_pe"], KC)
            load(RA, w_o[0].rearrange("(k p) n -> p k n", p=P), "wo_ld")
            load(WR, w_router[0].rearrange("(k p) e -> p k e", p=P), "router_ld")
            load(BR[0:1, :], b_router, "router_ld")

            def load_gu(par, e):
                load(BROW[32 * par:32 * par + 1, :], b_gate_up[0, e, :], f"wq{4 * par}")
                for k in range(0, KC, 2):
                    load(GU[par][:, k:k + 2, :], w_gate_up[0, e, k * P:(k + 2) * P, :].rearrange("a (k p) n -> p (a k) n", p=P), f"wq{4 * par + k // 2}")

            def load_dn(e, uses):
                for j in range(2):
                    if uses is not None:
                        sp.wait_ge(S["dnp_half" if j == 0 else "dnp"], uses)
                    for k in (2 * j, 4 + 2 * j):
                        load(DN[:, k:k + 2, :], w_down[0, e, k * P:(k + 2) * P, :].rearrange("a (k p) n -> p (a k) n", p=P), f"dn_ld{j}")

            def load_first(k):
                load(GU[0][:, k:k + 2, :], w_gate_up[0, 0:1, k * P:(k + 2) * P, :].rearrange("a (k p) n -> p (a k) n", p=P), f"wq{k // 2}")
            sp.wait_ge(S["pv_pe"], 2 * NP)
            sp.wait_ge(S["mod_row"], 2)
            sp.wait_ge(S["row_pe"], 6)
            load_first(0)
            sp.wait_ge(S["g2_pe"], 1)
            load_first(6)
            sp.wait_ge(S["a2_ok"], 1)
            sp.wait_ge(S["ys_zero"], 1)
            for h in range(2):
                load(YS_E[h * NB:h * NB + NE, :], b_down[0, :, h * BANK:(h + 1) * BANK], "bd_ld")
            sp.wait_ge(S["br_pe"], KC)
            load_first(2)
            load_first(4)
            load(BROW[0:1, :], b_gate_up[0, 0:1, :], "wq0")
            sp.wait_ge(S["wo_pe"], 2)
            load_gu(1, slice(1, 2))
            sp.wait_ge(S["h2_ok"], TT)
            sp.wait_ge(S["rt_pe"], 1)
            load_dn(slice(0, 1), None)
            sp.wait_ge(S["qs_ok"], 1)
            done = sp.value_load(qs_t[0:1, 1:2], min_val=1, max_val=4 * NE)
            load_dn(slice(1, 2), done)
            with sp.Fori(1, NE // 2) as pair:
                for par in range(2):
                    e = pair * 2 + par
                    two_ago = sp.value_load(qs_t[0:1, bass.ds(e - 1, 1)], min_val=1, max_val=4 * NE)
                    last_one = sp.value_load(qs_t[0:1, bass.ds(e, 1)], min_val=1, max_val=4 * NE)
                    sp.wait_ge(S["gup"], two_ago * 2)
                    load_gu(par, bass.ds(e, 1))
                    load_dn(bass.ds(e, 1), last_one)
            for t in range(TT):
                sp.wait_ge(S["fin"], t + 1)
                load(out[0, t * P:(t + 1) * P, :], X[:, t, :], "out_s")
            sp.wait_ge(S["out_s"], 16 * TT)

        @block.tensor
        def _(pe):
            mm, tp = pe.matmul, pe.transpose

            def need(name, n=1):
                pe.wait_ge(S[name], n)

            need("idn_ld", 16)
            need("vec_ld", 16 * 5)
            need("vec2_ld", 16 * 2)
            tp(PS[:, 7, 0:V_ROWS], VROWS[0:V_ROWS, :], IDN[0:V_ROWS, 0:V_ROWS]).then_inc(S["vec_t"], 1)
            need("lam_ld", 64)
            for r in range(2):
                last = tp(PS[:, 6, r * SG:(r + 1) * SG], LRAW[:, r, :], IDN[0:SG, 0:SG])
            last.then_inc(S["lam_t"], 1)
            def modulation(w, k, bank):
                for q in range(4):
                    last = mm(PS[32 * q:32 * q + 32, bank, :], SILU[:, k, :], w[:, q * BANK:(q + 1) * BANK],
                              start=(k == 0), stop=(k == KC - 1), tile_position=(0, 32 * q))
                return last

            def modulation_columns(third, bank):
                need("modr_ok", third + 1)
                for cc in range(4):
                    last = tp(PS[:, bank, cc * P:(cc + 1) * P], MODR[third][:, cc * P:(cc + 1) * P], IDN)
                last.then_inc(S["modt_pe"], 1)

            need("silu2")
            for k in range(KC):
                need(f"wq{k}", 16)
                last = modulation(WM0[:, k], k, 4)
            last.then_inc(S["mod0_pe"], 1)
            need("c_ld", 128)
            for r in range(2):
                for a in range(2):
                    last = tp(PS[:, 5, (r * 2 + a) * P:(r * 2 + a + 1) * P], CRAW[:, r, a, :], IDN)
            last.then_inc(S["ct_t"], 1)

            need("xn_ok", 4)
            for k in range(KC):
                if k >= 4:
                    need("ht_ok_a" if k % 2 == 0 else "ht_ok_v", (k - 4) // 2 + 1)
                for t in range(4):
                    last = tp(PS[:, k % 4, t * P:(t + 1) * P], XN[:, t, k * P:(k + 1) * P], IDN)
                last.then_inc(S["xnt_pe"], 1)
                if k == 3:
                    need("lam_ok"); need("ct_ok")
                    modulation_columns(0, 5)
            need("wu_ld", 16)
            for k in range(KC):
                need("ht_ok_a" if k % 2 == 0 else "ht_ok_v", k // 2 + 1)
                for m in range(2):
                    last = mm(PS[:, 6 + m, :], RA[:, k, m * P:(m + 1) * P], HT[:, k, :], start=(k == 0), stop=(k == KC - 1))
                    if k == KC - 1:
                        last.then_inc(S["u_pe"], 1)
            need("ra_ld", 16)
            for i in range(6):
                if i >= 4:
                    need("bcx_ok", i - 3)
                for k in range(KC):
                    last = mm(PS[:, i % 4, 0:T], RA[:, k, T + i * P:T + (i + 1) * P], HT[:, k, T:2 * T], start=(k == 0), stop=(k == KC - 1))
                last.then_inc(S["bcx_pe"], 1)
            RQ = view(odd_w, 8192, "", k=KC, n=768)
            need("rb_ld", 16)
            for t in range(TT):
                for k in range(KC):
                    last = mm(PS[:, 4, t * T:(t + 1) * T], HT[:, k, t * P:(t + 1) * P], RQ[:, k, 512:768], start=(k == 0), stop=(k == KC - 1))
            last.then_inc(S["kcx_pe"], 1)
            need("ut_ok", 2)
            need("bcx_ok", 6)
            for t in range(TT):
                for k in range(KC):
                    mm(PS[:, 6 + t, :], HT[:, k, T + t * P:T + (t + 1) * P], RQ[:, k, 0:512], start=(k == 0), stop=(k == KC - 1))
                    last = mm(PS[:, 5, t * T:(t + 1) * T], HT[:, k, T + t * P:T + (t + 1) * P], RQ[:, k, 512:768], start=(k == 0), stop=(k == KC - 1))
                last.then_inc(S["qk_pe"], 1)
            need("bcx_ok", 6)
            for j in range(L):
                for m in range(2):
                    last = tp(PS[0:NCH, j // 2, (j % 2) * T + m * P:(j % 2) * T + (m + 1) * P], UT[:, m, j::L], IDN)
            need("tabs_ok", 1)
            need("qk_ok", 4)
            need("kcx_ok", 2)
            for n in range(8):
                if n >= 4:
                    need("w1t_ok", n - 3)
                for i in range(4):
                    last = tp(PS[:, 4 + n % 4, i * P:(i + 1) * P], W1N[:, n // 4, (n % 4) * 4 + i, :, :].rearrange("p j h -> p (j h)"), IDN)
                last.then_inc(S["w1t_pe"], 1)
            need("uc_ok", 1)
            for g in range(SG):
                for r in range(2):
                    last = mm(PS[0:2 * SH, g // 4, (g % 4) * P:(g % 4 + 1) * P], BB[:, r, g, :, :].rearrange("p z h -> p (z h)"), CM[:, r, g, :], start=(r == 0), stop=(r == 1))
            last.then_inc(S["mz_pe"], 1)
            need("w1t_ok", 8)
            for g in range(SG):
                last = tp(PS[:, 4 + g // 8, (g % 8) * NCH:(g % 8 + 1) * NCH], UC[0:NCH, g, :, :].rearrange("p j h -> p (j h)"), IDN[0:NCH, 0:NCH])
            last.then_inc(S["u2_pe"], 1)
            need("ra_ld", 80)
            for k in range(4):
                last = modulation(RAM[:, k], k, 6)
            last.then_inc(S["ra_free"], 1)
            need("rb_ld", 80)
            for k in range(4):
                last = modulation(RBM[:, k], 4 + k, 6)
            last.then_inc(S["rb_free"], 1)
            need("u2_ok", 1)
            need("qp_ok", 1)
            need("mod_row", 1)
            for t in range(TT):
                for i in range(NP):
                    last = tp(PS[:, 4 + i // 2, (i % 2) * T + t * P:(i % 2) * T + (t + 1) * P], QP[:, t, i, :], IDN)
            for t in range(TT):
                last = tp(PS[:, 6, T + t * P:T + (t + 1) * P], QP[:, t, NP, :], IDN)
            for t in range(TT):
                last = tp(PS[:, 6, t * P:(t + 1) * P], KCX[:, t, :, :].rearrange("p h d -> p (h d)"), IDN)
            last.then_inc(S["qt_pe"], 1)
            need("u2_ok", 1)
            need("mz_ok", 1)
            for r in range(2):
                for g in range(SG):
                    last = mm(PS[:, r * 2 + g // 8, (g % 8) * NCH:(g % 8 + 1) * NCH], W1T[:, r, g, :], U2[:, g, :], start=True, stop=True)
            last.then_inc(S["inc_pe"], 1)

            def turn_probabilities(n):
                need("p_ok", n + 1)
                if n:
                    need("pt_ok", n)
                for kc in range(4):
                    for g in range(2):
                        last = tp(PS[:, 4 + kc // 2, (kc % 2) * T + g * P:(kc % 2) * T + (g + 1) * P], PR[:, n % 2, g, kc * P:(kc + 1) * P], IDN)
                last.then_inc(S["pt_pe"], 1)

            def by_values(n):
                need("pt_ok", n + 1)
                need("g_sg", n + 1)
                for kc in range(4):
                    for g in range(2):
                        last = mm(PS[g * HD:(g + 1) * HD, 3, T:T + P], VV[:, kc, g * HD:(g + 1) * HD], PT[:, kc, g * P:(g + 1) * P], start=(kc == 0), stop=(kc == 3), tile_position=(0, g * HD))
                last.then_inc(S["pv_pe"], 1)

            def gates(m):
                need(f"g_ld{m % 3}", 48 * (m // 3 + 1))
                if m:
                    need("g_sg", m)
                for s_ in range(3):
                    if s_ == 2 and m:
                        need("yat_ok", m)
                    for k in range(KC):
                        last = mm(PS[:, 2 + s_ // 2, (s_ % 2) * T:(s_ % 2 + 1) * T], RG[m % 3][:, k, s_, :], HT[:, k, T:2 * T], start=(k == 0), stop=(k == KC - 1))
                last.then_inc(S["g_pe"], 1)

            def ssm_output(quarter):
                if quarter == 0:
                    need("zr_ok", 1)
                else:
                    need("yc_ok", quarter)
                for g in range(4 * quarter, 4 * quarter + 4):
                    o = PS[0:CCH, 7, (g % 4) * P:(g % 4 + 1) * P]
                    mm(o, U2[:, g, CCH:NCH], TZ[:, g, :], start=True, stop=False)
                    mm(o, ZR[:, 0, g, :], CM[:, 0, g, :], start=False, stop=False)
                    last = mm(o, ZR[:, 1, g, :], CM[:, 1, g, :], start=False, stop=True)
                last.then_inc(S["y_pe"], 1)

            need("qt_ok", 2)
            need("zs_ok", 2)
            need("tz_ld", 16 * 15)

            def scores(n):
                t, i = n // NP, n % NP
                if n:
                    need("s_ok", n)
                for g in range(2):
                    last = mm(PS[:, g, :], QT[:, i, t * P:(t + 1) * P], KT[:, g, :], start=True, stop=True)
                last.then_inc(S["s_pe"], 1)

            scores(0)
            for n in range(2 * NP):
                gates(n)
                need("wm2_ld", 16 * (n + 1))
                modulation(WM2, n, 6).then_inc(S["wm2_pe"], 1)
                if n >= 4:
                    ssm_output(n - 4)
                turn_probabilities(n)
                if n + 1 < 2 * NP:
                    scores(n + 1)
                by_values(n)

            def row(i, q, bank):
                return mm(PS[:, bank, :], ROWSEL[:, q, :], MODR[i], start=True, stop=True)

            need("yc_ok", 4)
            for m in range(2):
                for j in range(L):
                    last = tp(PS[:, 7, m * T + j * CCH:m * T + (j + 1) * CCH], YC[0:CCH, j, m * P:(m + 1) * P], IDN[0:CCH, 0:CCH])
            last.then_inc(S["yt_pe"], 1)
            need("g_sg", KC)
            need("mod_row", 2)
            need("rowsel_ok", 1)
            for i, q, bank in ((2, 0, 4), (2, 1, 5), (1, 0, 0), (1, 1, 1), (1, 2, 2), (1, 3, 3)):
                if bank == 3:
                    need("yat_ok", 2 * NP)
                row(i, q, bank).then_inc(S["row_pe"], 1)
            need("br_ld", 64)
            need("yat_ok", 2 * NP)
            need("yconv_ok", 1)

            def two_branches(m):
                b = 4 + 2 * (m % 2)
                for k in range(2):
                    mm(PS[:, b, T:2 * T], CONVO[:, k, m * P:(m + 1) * P], YCONV[:, k, :], start=(k == 0), stop=(k == 1))
                for k in range(NP):
                    mm(PS[:, b + 1, 0:T], ATTO[:, k, m * P:(m + 1) * P], YAT[:, k, :], start=(k == 0), stop=(k == NP - 1))

            def out_projection(t, k):
                for h in range(2):
                    last = mm(PS[:, 2 * t + h, :], MERG[:, k, t * P:(t + 1) * P], RA[:, k, h * BANK:(h + 1) * BANK], start=(k == 0), stop=(k == KC - 1))
                return last

            need("row_ok", 1)
            two_branches(0)
            need("gelu_in", 1)
            two_branches(1)
            need("wglu_ld", 16)
            need("z_ok", 1)
            need("row_ok", 3)
            for m in range(2):
                for k in range(2):
                    last = mm(PS[:, 3, m * T:(m + 1) * T], WGLU[:, k, m * P:(m + 1) * P], YS[:, k, :], start=(k == 0), stop=(k == 1))
            last.then_inc(S["glu_pe"], 1)
            for q in range(2):
                last = row(2, 2 + q, 1 + q)
            last.then_inc(S["g2_pe"], 1)
            need("yssm_ok", 1)
            for m in range(KC):
                if m >= 2:
                    need("merg_ok", m - 1)
                    two_branches(m)
                for k in range(2):
                    last = mm(PS[:, 4 + 2 * (m % 2), 0:T], SSMO[:, k, m * P:(m + 1) * P], YA[:, k, :], start=(k == 0), stop=(k == 1))
                last.then_inc(S["br_pe"], 1)
                if m == 1:
                    need("wo_ld", 16)
                    need("row_ok", 4)
                if m:
                    need("merg_ok", m)
                    out_projection(0, m - 1)
            need("merg_ok", KC)
            out_projection(0, KC - 1).then_inc(S["wo_pe"], 1)
            for k in range(KC):
                last = out_projection(1, k)
            last.then_inc(S["wo_pe"], 1)
            need("router_ld", 32)
            for t in range(TT):
                need("h2_ok", t + 1)
                for k in range(KC):
                    last = tp(PS[:, 6 - 6 * t + k // 4, (k % 4) * P:(k % 4 + 1) * P], H2[:, t, k * P:(k + 1) * P], IDN)
                last.then_inc(S["h2t_pe"], 1)
                need("h2t_ok", t + 1)
                for k in range(KC):
                    mm(PS[:, 4, t * 64:t * 64 + NE], H2T[:, k, t * P:(t + 1) * P], WR[:, k, :], start=(k == 0), stop=False)
                last = mm(PS[:, 4, t * 64:t * 64 + NE], ONES[0:1, :], BR[0:1, :], start=False, stop=True)
            last.then_inc(S["rt_pe"], 1)
            need("const", 32)
            need("mk_ok", 1)
            mm(PS[:, 7, 0:NE], BEF, MK[:, 0, :], start=True, stop=True)
            mm(PS[:, 7, 64:64 + NE], ONES, MK[:, 0, :], start=True, stop=False)
            mm(PS[:, 7, 64:64 + NE], BEF, MK[:, 1, :], start=False, stop=True)
            mm(PS[0:NE, 7, 128:129], MK[:, 0, :], ONES[:, 0:1], start=True, stop=False)
            last = mm(PS[0:NE, 7, 128:129], MK[:, 1, :], ONES[:, 0:1], start=False, stop=True)
            last.then_inc(S["pos_pe"], 1)
            need("gm_ok", 1)
            for t in range(TT):
                for h in range(2):
                    last = mm(PS[h * NB:h * NB + NE, 5, t * P:(t + 1) * P], GM[:, t, :], IDN, start=True, stop=True, tile_position=(0, h * NB))
            last.then_inc(S["gt_pe"], 1)
            need("tab", 1)
            mm(PS[0:1, 6, 0:NE + 1], NBK[0:NE, :], BEF[0:NE, 0:NE + 1], start=True, stop=True).then_inc(S["qs_pe"], 1)
            def gather():
                for t in range(TT):
                    for h in range(2):
                        last = mm(PS[h * NB:(h + 1) * NB, 6, :], SEL[:, t, :], H2[:, t, h * BANK:(h + 1) * BANK], start=(t == 0), stop=(t == 1))
                last.then_inc(S["gathered"], 1)

            def turn_tokens():
                for i in range(4):
                    last = tp(PS[:, 4 + i // 2, T + (i % 2) * P:T + (i % 2 + 1) * P], XS[:, i * P:(i + 1) * P], IDN)
                last.then_inc(S["xt"], 1)

            def scatter():
                for t in range(TT):
                    for h in range(2):
                        last = mm(PS[:, 2 * t + h, :], SELGT[:, h, t * P:(t + 1) * P], YS_E, start=False, stop=True, skip_group_check=True)
                    last.then_inc(S["scat"], 1)

            def turn_act(q, j):
                pe.wait_ge(S["act"], 2 * q + j + 1)
                for i in range(2):
                    last = tp(PS[:, 4 + j, i * P:(i + 1) * P], ACTA[:, j * T + i * P:j * T + (i + 1) * P], IDN)
                last.then_inc(S["atp"], 1)

            need("qs_ok", 1)
            need("sel", 1)
            gather()
            need("xs", 1)
            need("gt_ok", 1)
            turn_tokens()
            need("bd_ld", 32)
            with pe.Fori(0, NE // 2) as pair:
                for par in range(2):
                    e = pair * 2 + par
                    first = pe.value_load(qs_t[0:1, bass.ds(e, 1)], min_val=0, max_val=4 * NE)
                    end = pe.value_load(qs_t[0:1, bass.ds(e + 1, 1)], min_val=1, max_val=4 * NE)
                    with pe.Fori(first, end) as q:
                        def gate_up(j, ks):
                            for k in ks:
                                if j == 0 and k % 2 == 0:
                                    pe.wait_ge(S[f"wq{4 * par + k // 2}"], (pair + 1) * (32 if k == 0 else 16) + 16)
                                for h in range(2):
                                    mm(PS[h * NB:(h + 1) * NB, 4 + j, :], XG[:, k % 4, (k // 4) * NB:(k // 4 + 1) * NB],
                                       GU[par][:, k, h * F + j * BANK:h * F + (j + 1) * BANK], start=(k == 0), stop=False)

                        def gate_up_bias(j):
                            for h in range(2):
                                last = mm(PS[h * NB:(h + 1) * NB, 4 + j, :], ONES[32 * par:32 * par + 1, 0:NB],
                                          BROW[32 * par:32 * par + 1, h * F + j * BANK:h * F + (j + 1) * BANK], start=False, stop=True)
                            last.then_inc(S["gup"], 1)

                        def down(j):
                            pe.wait_ge(S["at"], 2 * q + j + 1)
                            pe.wait_ge(S[f"dn_ld{j}"], (e + 1) * 32)
                            for i in range(2):
                                for hh in range(2):
                                    for h in range(2):
                                        last = mm(PS[h * NB:(h + 1) * NB, 7, :], ACTT[:, 2 * j + i, hh * NB:(hh + 1) * NB],
                                                  DN[:, hh * 4 + 2 * j + i, h * BANK:(h + 1) * BANK],
                                                  start=(j + i + hh == 0), stop=(j + i + hh == 3))
                            last.then_inc(S["dnp_half" if j == 0 else "dnp"], 1)

                        pe.wait_ge(S["yc"], q + 1)
                        for t in range(TT):
                            for h in range(2):
                                last = mm(PS[h * NB:(h + 1) * NB, 7, t * P:(t + 1) * P], SELG[:, t, :], IDN, start=True, stop=True)
                        last.then_inc(S["selgt"], 1)
                        pe.wait_ge(S["xg"], q + 1)
                        gate_up(0, range(4))
                        scatter()
                        gate_up(0, range(4, KC))
                        gate_up_bias(0)
                        gate_up(1, range(4))
                        turn_act(q, 0)
                        gate_up(1, range(4, KC))
                        gate_up_bias(1)
                        pe.wait_ge(S["selgtc"], (q + 1) * 2)
                        down(0)
                        turn_act(q, 1)
                        pe.wait_ge(S["sel"], q + 2)
                        gather()
                        down(1)
                        pe.wait_ge(S["xs"], q + 2)
                        turn_tokens()
            blocks = pe.value_load(qs_t[0:1, NE:NE + 1], min_val=1, max_val=4 * NE)
            pe.wait_ge(S["yc"], blocks + 1)
            scatter()

        @block.scalar
        def _(act):
            n = [0]

            def do(ins):
                n[0] += 1
                return ins.then_inc(S["act_s"], 1)

            def settle():
                act.wait_ge(S["act_s"], n[0])

            def tell(name, k=1):
                settle()
                act.sem_inc(S[name], k)

            def need(name, k=1):
                act.wait_ge(S[name], k)

            def load(dst, src, name):
                act.dma_start(dst, src).then_inc(S[name], 16)

            def copy(dst, src):
                return do(act.activation(dst, src, ACT.Copy))

            for t in range(TT):
                load(CX[:, t, :], ctx[0, t * P:(t + 1) * P, :], "x_ld")
                load(X[:, t, :], x[0, t * P:(t + 1) * P, :], "x_ld")
            for z in range(2):
                load(LAM[z * SS:(z + 1) * SS, 0, :], ssm_log_dt[0, z:z + 1, :].to_broadcast([SS, SG]), "lam_ld")
            for r, v in enumerate((ssm_lam_re, ssm_lam_im)):
                load(LRAW[:, r, :].rearrange("g (z s) -> g z s", z=2), v[0].rearrange("z g s -> g z s"), "lam_ld")
            load(SINKS, attn_sinks.to_broadcast([P, NQ]), "qk_ld")
            load(QKG[:, 0, :], q_norm_g.to_broadcast([P, HD]), "qk_ld")
            load(QKG[:, 1, :], k_norm_g.to_broadcast([P, HD]), "qk_ld")
            load(COS, cosine.rearrange("(t p) d -> p t d", p=P), "qk_ld")
            load(SIN, sine.rearrange("(t p) d -> p t d", p=P), "qk_ld")
            load(MASK, window.rearrange("(t p) k -> p t k", p=P), "mask_ld")
            need("vec_ok")
            do(act.activation(SIG16, VEC[:, V_C:V_C + 16], ACT.Sigmoid))
            tell("silu_ok")
            need("lam_ld", 64)
            do(act.activation(LAM[:, 1, :], LAM[:, 0, :], ACT.Exp))
            tell("dt_ok")
            need("x_ld", 64)
            for i, src in enumerate((CX[:, 0, :], CX[:, 1, :], X[:, 0, :], X[:, 1, :])):
                do(act.activation(XN[:, i, :], src, ACT.Square, accum_out=STAT[:, i:i + 1]))
            tell("sq_sum")
            need("sd_ok")
            do(act.activation(STAT[:, 8:12], STAT[:, 4:8], ACT.Sqrt))
            tell("stat_ok")

            need("mod0_pe")
            copy(MODR[0], PS[:, 4, :])
            tell("modr_ok")
            need("mod_ok", 1)
            for k in range(0, KC, 2):
                need("xnt_pe", k + 1)
                do(act.activation(HT[:, k, T:2 * T], PS[:, k % 4, T:2 * T], ACT.Identity, bias=MOD[:, 0, k, 0:1], scale=A1[:, k, 0:1]))
                do(act.activation(HT[:, k, 0:T], PS[:, k % 4, 0:T], ACT.Identity, bias=MOD[:, 0, k, 1:2], scale=A1[:, k, 1:2]))
                tell("ht_ok_a")
            for m in range(2):
                need("u_pe", m + 1)
                copy(UT[:, m, :], PS[:, 6 + m, :])
                tell("ut_ok")
            for i in range(6):
                need("bcx_pe", i + 1)
                copy(BCX[:, i, :], PS[:, i % 4, 0:T])
                tell("bcx_ok")
            need("kcx_pe")
            need("xnt_pe", KC)
            kv = PS[:, 4, :].rearrange("p (t n) -> p t n", t=TT)
            copy(KCX[:, :, :, :].rearrange("p t h d -> p t (h d)"), kv[:, :, 0:P])
            tell("kcx_ok")
            copy(VV[:, 0:2, :], kv[:, :, P:2 * P])
            tell("kcx_ok")
            for t in range(TT):
                need("qk_pe", t + 1)
                copy(QK[:, t, 0:NQ, :].rearrange("p (i g) d -> p g i d", g=2), PS[:, 6 + t, :].rearrange("p (g i d) -> p g i d", g=2, i=NP))
                tell("qk_ok")
            kv = PS[:, 5, :].rearrange("p (t n) -> p t n", t=TT)
            copy(QK[:, :, NQ:NQ + NKV, :].rearrange("p t h d -> p t (h d)"), kv[:, :, 0:P])
            copy(VV[:, 2:4, :], kv[:, :, P:2 * P])
            tell("qk_ok", 2)
            for i in range(8):
                need("w1t_pe", i + 1)
                copy(W1T[:, i // 4, (i % 4) * 4:(i % 4) * 4 + 4, :].rearrange("p g s -> p (g s)"), PS[:, 4 + i % 4, :])
                tell("w1t_ok")
                if i == 3:
                    need("w1t_pe", 8)
                    for b in range(4):
                        copy(UC[0:NCH, :, 2 * b:2 * b + 2, :].rearrange("p g j h -> p j g h"), PS[0:NCH, b, :].rearrange("p (j g h) -> p j g h", j=2, g=SG))
                    tell("uc_ok")
            need("qss")
            do(act.activation(QST[:, 0:24], QST[:, 24:48], ACT.Sqrt))
            tell("qrs")
            need("mz_pe")
            copy(MZ[0:2 * SH, :, :].rearrange("p (b g) j -> p b (g j)", b=4), PS[0:2 * SH, 0:4, :])
            tell("mz_ok")
            need("qt_pe")
            need("tz_ld", 16 * 15)
            copy(QT[:, :, :].rearrange("p (b i) t -> p b (i t)", b=2), PS[:, 4:6, :])
            tell("qt_ok")
            need("inc_pe")
            for r in range(2):
                for c0 in (0, CCH):
                    dst = ZS[SS:P, r, :, c0:c0 + CCH]
                    src = PS[SS:P, 2 * r:2 * r + 2, :].rearrange("p b (g c) -> p (b g) c", c=NCH)
                    src = src[:, :, c0 + CCH - 1::-1] if c0 == 0 else src[:, :, NCH - 1:CCH - 1:-1]
                    copy(dst, src)
            tell("zs_ok")

            def probs_turned(n):
                need("pt_pe", n + 1)
                if n:
                    need("pv_pe", n)
                copy(PT[:, :, :].rearrange("p (b c) q -> p b (c q)", b=2), PS[:, 4:6, :])
                tell("pt_ok")
                need("pv_pe", n + 1)
                copy(YAT[:, n % NP, (n // NP) * P:(n // NP + 1) * P], PS[:, 3, T:T + P])
                tell("yat_ok")

            for n_ in range(2 * NP):
                need("smax", n_ + 1)
                i = n_ % 2
                for g in range(2):
                    do(act.activation(PR[:, i, g, :], PR[:, i, g, :], ACT.Exp, bias=AC[:, i, 2 + g:3 + g], accum_out=AC[:, i, 6 + g:7 + g]))
                do(act.activation(AC[:, i, 4:6], AC[:, i, 8:10], ACT.Exp))
                tell("sexp")
                need("g_pe", n_ + 1)
                do(act.activation(SG_[:, n_, 0:2, :], PS[:, 2, :].rearrange("p (s t) -> p s t", s=2), ACT.Sigmoid))
                do(act.activation(SG_[:, n_, 2, :], PS[:, 3, 0:T], ACT.Sigmoid))
                tell("g_sg")
                if n_ >= 4:
                    b = n_ - 4
                    need("y_pe", b + 1)
                    copy(YC[0:CCH, :, b * 64:(b + 1) * 64].rearrange("p j (g h) -> p g j h", g=4), PS[0:CCH, 7, :].rearrange("p (g j h) -> p g j h", g=4, j=L))
                    tell("yc_ok")
                probs_turned(n_)
            for i, (dst, b) in enumerate(((A2ROW, 4), (G1ROW, 0), (S2ROW, 2))):
                need("row_pe", 2 * i + 2)
                copy(dst[:, :].rearrange("p (b n) -> p b n", b=2), PS[:, b:b + 2, :])
                tell("row_ok")
                if i == 1:
                    need("gelu_in")
                    do(act.activation(YG[:, :], YT1[:, :], ACT.Sigmoid, scale=GELU_S))
                    tell("gelu_sg")
            need("glu_pe")
            do(act.activation(YG[:, :], PS[:, 3, :], ACT.Sigmoid))
            tell("glu_ok")
            need("g2_pe")
            copy(G2ROW[:, :].rearrange("p (b n) -> p b n", b=2), PS[:, 1:3, :])
            tell("row_ok")
            for t in range(TT):
                need("x1_ok", t + 1)
                do(act.activation(SQ2, X[:, t, :], ACT.Square, accum_out=STAT[:, t:t + 1]))
                tell("ss2")
                need("ss2_ok", t + 1)
                do(act.activation(STAT[:, 8 + t:9 + t], STAT[:, 4 + t:5 + t], ACT.Sqrt))
                tell("sd2")
                need("h2t_pe", t + 1)
                b = 6 - 6 * t
                copy(H2T[:, :, t * P:(t + 1) * P].rearrange("p (b k) t -> p b k t", b=2), PS[:, b:b + 2, :].rearrange("p b (k t) -> p b k t", t=P))
                tell("h2t_ok")
            need("ex_in")
            for t in range(TT):
                do(act.activation(E4[:, t, 0:4], V8[:, t, 0:4], ACT.Exp, bias=NV0[:, t:t + 1], accum_out=ESUM[:, t:t + 1]))
            tell("ex_out")
            need("qs_ok")
            need("gathered")
            act.activation(XS, PS[:, 6, :], ACT.Copy).then_inc(S["xs"], 1)
            blocks = act.value_load(qs_t[0:1, NE:NE + 1], min_val=1, max_val=4 * NE)
            with act.Fori(0, blocks) as q:
                act.wait_ge(S["scat"], (q + 1) * 2)
                for h in range(2):
                    act.activation(SELGT[h * NB:(h + 1) * NB, h, :], PS[h * NB:(h + 1) * NB, 7, 0:T], ACT.Copy).then_inc(S["selgtc"], 1)
                for j in range(2):
                    s = slice(j * T, (j + 1) * T)
                    act.wait_ge(S["glu"], 2 * q + j + 1)
                    act.activation(ACTA[:, s], GL[:, s], ACT.Sigmoid, scale=ALPHA).then_inc(S["sg"], 1)
                    act.wait_ge(S["atp"], 2 * q + j + 1)
                    act.activation(act_t[:, s], PS[:, 4 + j, 0:T], ACT.Copy).then_inc(S["at"], 1)
                act.wait_ge(S["gathered"], q + 2)
                act.activation(XS, PS[:, 6, :], ACT.Copy).then_inc(S["xs"], 1)
                act.wait_ge(S["dnp"], q + 1)
                act.activation(YS_E, PS[:, 7, :], ACT.Copy).then_inc(S["yc"], 1)

        @block.gpsimd
        def _(pool):
            n = [0]

            def do(ins):
                n[0] += 1
                return ins.then_inc(S["pool"], 1)

            def settle():
                pool.wait_ge(S["pool"], n[0])

            def tell(name, k=1):
                settle()
                pool.sem_inc(S[name], k)

            def need(name, k=1):
                pool.wait_ge(S[name], k)

            def load(dst, src, name):
                pool.dma_start(dst, src).then_inc(S[name], 16)

            load(VROWS[V_CCTX:V_CCTX + KC, :], c_ctx.rearrange("(k p) -> k p", p=P), "vec2_ld")
            load(VROWS[V_TAPS:V_TAPS + 6, :], conv_w[0].rearrange("w (k p) -> (w k) p", p=P), "vec2_ld")
            load(BEF, before, "const")
            load(IOTA, iota, "const")
            for r, v in enumerate((ssm_c_re, ssm_c_im)):
                for a in range(2):
                    for z in range(2):
                        load(CRAW[:, r, a, z * SS:(z + 1) * SS], v[0, z, a * 8:(a + 1) * 8].rearrange("g h s -> (g h) s"), "c_ld")
            for r, v in enumerate((ssm_b_re, ssm_b_im)):
                for z in range(2):
                    load(BRAW[z * SS:(z + 1) * SS, r, :, :], v[0, z].rearrange("g s h -> s g h"), "braw_ld")
            need("mod0_pe")
            do(pool.memset(TZ, 0.0))
            settle()
            tell("tz_zero")
            need("zs_ok", 2)
            need("u2_ok")
            T1, T2 = SCT

            def grow(dst, src, k, shape):
                free = [P] + shape
                n_ = int(np.prod(shape))
                names = " ".join("abc"[:len(shape)])
                t1, t2 = (t[:, 0:n_].rearrange(f"p ({names}) -> p {names}", **dict(zip("abc", shape))) for t in (T1, T2))
                do(pool.tensor_tensor(t1, PAR[:, k, :, :].unsqueeze(3).to_broadcast(free), src, ALU.mult))
                do(pool.tensor_tensor(t2, PAI[:, k, :, :].unsqueeze(3).to_broadcast(free), src[:, ::-1], ALU.mult))
                settle()
                do(pool.tensor_tensor(dst, dst, t1, ALU.add))
                settle()
                do(pool.tensor_tensor(dst, dst, t2, ALU.add))
                settle()

            for lev in range(5):
                st = 2 ** (lev + 1)
                cnt = CCH // st
                grow(ZS[:, :, :, st - 1:CCH:st], ZS[:, :, :, st // 2 - 1:CCH:st], lev, [2, SG, cnt])
            for i in range(1, 8):
                grow(ZS[:, :, :, CCH + i:NCH:8], ZS[:, :, :, CCH + i - 1:NCH:8], 0, [2, SG, 4])
            carry = [31, 3, 7, 11]
            for s_ in range(3):
                do(pool.tensor_copy(ZS[:, :, :, carry[s_ + 1]:carry[s_ + 1] + 1], ZS[:, :, :, CCH + 8 * s_ + 7:CCH + 8 * s_ + 8]))
                settle()
                grow(ZS[:, :, :, carry[s_ + 1]:carry[s_ + 1] + 1], ZS[:, :, :, carry[s_]:carry[s_] + 1], 3, [2, SG, 1])
            for s_ in range(4):
                base = CCH + 8 * s_
                C = ZS[:, :, :, carry[s_]:carry[s_] + 1]
                for r in range(2):
                    shape = [P, SG, 7]
                    zc = C[:, r].to_broadcast(shape)
                    zo = C[:, 1 - r].to_broadcast(shape)
                    t1 = T1[:, r * 128:r * 128 + 112].rearrange("p (g i) -> p g i", g=SG)
                    t2 = T2[:, r * 128:r * 128 + 112].rearrange("p (g i) -> p g i", g=SG)
                    do(pool.tensor_tensor(t1, PA[:, 0, 0:7, :].rearrange("p k g -> p g k"), zc, ALU.mult))
                    do(pool.tensor_tensor(t2, PA[:, 1, 0:7, :].rearrange("p k g -> p g k"), zo, ALU.mult))
                    settle()
                    w = ZS[:, r, :, base:base + 7]
                    do(pool.tensor_tensor(t1, t1, t2, ALU.subtract if r == 0 else ALU.add))
                    settle()
                    do(pool.tensor_tensor(w, w, t1, ALU.add))
            tell("scan_ok")
            need("qt_pe")
            do(pool.memset(ROWSEL, 0.0))
            settle()
            for q in range(4):
                do(pool.memset(ROWSEL[32 * q:32 * q + 1, q, :], 1.0))
            tell("rowsel_ok")
            need("pv_pe", 2 * NP)
            need("p_ok", 2 * NP)
            do(pool.memset(YS_E, 0.0))
            tell("ys_zero")
            need("rt_pe")
            do(pool.memset(SELGT, 0.0))
            tell("yc")

        @block.vector
        def _(ve):
            n = [0]

            def do(ins):
                n[0] += 1
                return ins.then_inc(S["dve"], 1)

            def settle():
                ve.wait_ge(S["dve"], n[0])

            def tell(name, k=1):
                settle()
                ve.sem_inc(S[name], k)

            def need(name, k=1):
                ve.wait_ge(S[name], k)

            def tt(dst, a, b, op):
                return do(ve.tensor_tensor(dst, a, b, op))

            def ts(dst, a, s1, s2, op0, op1=ALU.bypass):
                return do(ve.tensor_scalar(dst, a, s1, s2, op0) if op1 == ALU.bypass else ve.tensor_scalar(dst, a, s1, s2, op0, op1))

            def stt(dst, a, sc, b, op0, op1):
                return do(ve.scalar_tensor_tensor(out=dst, in0=a, scalar=sc, in1=b, op0=op0, op1=op1))

            def copy(dst, src):
                return do(ve.tensor_copy(dst, src))

            do(ve.memset(ONES, 1.0))
            do(ve.memset(silu_t[:, :], 0.0))
            settle()
            need("vec_t")
            copy(VEC[:, :], PS[:, 7, 0:V_ROWS])
            tell("vec_ok")
            need("silu_ok")
            tt(SILU[:, :, 0:2], VEC[:, V_C:V_C + 16].rearrange("p (v k) -> p k v", v=2), SIG16.rearrange("p (v k) -> p k v", v=2), ALU.mult)
            tell("silu2")
            need("sq_sum")
            ts(STAT[:, 4:8], STAT[:, 0:4], 1.0 / D, EPS, ALU.mult, ALU.add)
            tell("sd_ok")
            need("stat_ok")
            do(ve.reciprocal(STAT[:, 12:16], STAT[:, 8:12]))
            settle()
            for i, src in enumerate((CX[:, 0, :], CX[:, 1, :], X[:, 0, :], X[:, 1, :])):
                ts(XN[:, i, :], src, STAT[:, 12 + i:13 + i], None, ALU.mult)
            tell("xn_ok", 4)
            need("lam_t")
            copy(LAM[:, 2:4, :], PS[:, 6, 0:2 * SG].rearrange("p (r g) -> p r g", r=2))
            tell("lam_ok")
            need("ct_t")
            copy(CT[:, :, :, :].rearrange("p r g h -> p (r g h)"), PS[:, 5, :])
            tell("ct_ok")

            def modulation_columns(third, bank):
                need("modt_pe", third + 1)
                src = PS[:, bank, :].rearrange("p (c q m) -> p q c m", c=4, q=4)[:, :, :, 0:2]
                dst = MOD[:, 2 * third:2 * third + 2, :, :].rearrange("p w (a c) v -> p (w a) c v", c=4)
                bias = VEC[:, V_BMOD + 16 * third:V_BMOD + 16 * third + 16].rearrange("p (q c) -> p q c", c=4).unsqueeze(3).to_broadcast([P, 4, 4, 2])
                tt(dst, src, bias, ALU.add)
                settle()

            modulation_columns(0, 5)
            stt(A1[:, :, :], MOD[:, 1, :, :], 1.0, VEC[:, V_N1:V_N1 + KC].unsqueeze(2).to_broadcast([P, KC, 2]), ALU.add, ALU.mult)
            tell("mod_ok")
            for k in range(1, KC, 2):
                need("xnt_pe", k + 1)
                ts(HT[:, k, T:2 * T], PS[:, k % 4, T:2 * T], A1[:, k, 0:1], MOD[:, 0, k, 0:1], ALU.mult, ALU.add)
                ts(HT[:, k, 0:T], PS[:, k % 4, 0:T], A1[:, k, 1:2], MOD[:, 0, k, 1:2], ALU.mult, ALU.add)
                tell("ht_ok_v")

            L_ = [LAM[:, i, :] for i in range(20)]
            lre, lim, xr, yi, m, t, kk, sn, cm, t2, nr, ni, ar, ai, den, br_, bi_ = L_[2:19]
            dt = L_[1]
            need("dt_ok")
            tt(xr, lre, dt, ALU.mult)
            tt(yi, lim, dt, ALU.mult)
            settle()
            ts(xr, xr, -104.0, 104.0, ALU.max, ALU.min)
            ts(kk, yi, 1.0 / TWO_PI, ROUND, ALU.mult, ALU.add)
            settle()
            ts(xr, xr, 1.0 / 256, None, ALU.mult)
            ts(kk, kk, -ROUND, None, ALU.add)
            settle()
            ts(m, xr, 1.0 / 7, 1.0, ALU.mult, ALU.add)
            stt(yi, kk, -PI_A, yi, ALU.mult, ALU.add)
            settle()
            for d in (6, 5, 4, 3, 2):
                tt(m, m, xr, ALU.mult)
                if d == 6:
                    stt(yi, kk, -PI_B, yi, ALU.mult, ALU.add)
                if d == 5:
                    stt(yi, kk, -PI_C, yi, ALU.mult, ALU.add)
                if d == 4:
                    ts(yi, yi, 0.25, None, ALU.mult)
                if d == 3:
                    tt(t2, yi, yi, ALU.mult)
                settle()
                ts(m, m, 1.0 / d, 1.0, ALU.mult, ALU.add)
                settle()
            tt(m, m, xr, ALU.mult)
            settle()
            for _ in range(8):
                stt(m, m, 2.0, m, ALU.add, ALU.mult)
                settle()
            ts(sn, t2, -1.0 / 110, 1.0, ALU.mult, ALU.add)
            ts(cm, t2, -1.0 / 132, 1.0, ALU.mult, ALU.add)
            settle()
            for ds, dc in ((72, 90), (42, 56), (20, 30), (6, 12)):
                tt(sn, sn, t2, ALU.mult)
                tt(cm, cm, t2, ALU.mult)
                settle()
                ts(sn, sn, -1.0 / ds, 1.0, ALU.mult, ALU.add)
                ts(cm, cm, -1.0 / dc, 1.0, ALU.mult, ALU.add)
                settle()
            tt(sn, sn, yi, ALU.mult)
            stt(cm, cm, -0.5, t2, ALU.mult, ALU.mult)
            settle()
            for _ in range(2):
                stt(t, cm, 1.0, sn, ALU.add, ALU.mult)
                tt(t2, sn, sn, ALU.mult)
                settle()
                ts(sn, t, 2.0, None, ALU.mult)
                ts(cm, t2, -2.0, None, ALU.mult)
                settle()
            stt(nr, cm, 1.0, m, ALU.add, ALU.mult)
            stt(ni, m, 1.0, sn, ALU.add, ALU.mult)
            settle()
            tt(nr, nr, cm, ALU.add)
            tt(t, lre, lre, ALU.mult)
            tt(t2, lim, lim, ALU.mult)
            settle()
            ts(POW[:, 0, 0, :], nr, 1.0, None, ALU.add)
            copy(POW[:, 1, 0, :], ni)
            tt(den, t, t2, ALU.add)
            tt(br_, nr, lre, ALU.mult)
            tt(ar, ni, lim, ALU.mult)
            settle()
            do(ve.reciprocal(den, den))
            tt(br_, br_, ar, ALU.add)
            tt(bi_, ni, lre, ALU.mult)
            tt(ai, nr, lim, ALU.mult)
            settle()
            tt(bi_, bi_, ai, ALU.subtract)
            tt(br_, br_, den, ALU.mult)
            settle()
            tt(bi_, bi_, den, ALU.mult)
            settle()

            def cmul(dr, di, ar, ai, br, bi, tmp, negate=False):
                t0, t1, t2, t3 = tmp
                tt(t0, ar, br, ALU.mult)
                tt(t1, ai, bi, ALU.mult)
                tt(t2, ar, bi, ALU.mult)
                tt(t3, ai, br, ALU.mult)
                settle()
                tt(dr, t0, t1, ALU.subtract)
                if negate:
                    stt(di, t2, -1.0, t3, ALU.mult, ALU.subtract)
                else:
                    tt(di, t2, t3, ALU.add)
                settle()

            small = [even_w[:, 4096 + 256 * i:4096 + 256 * (i + 1)] for i in range(4)]

            def temps(shape):
                n_ = int(np.prod(shape))
                names = " ".join("abc"[:len(shape)])
                return [s[:, 0:n_].rearrange(f"p ({names}) -> p {names}", **dict(zip("abc", shape))) for s in small]

            def powers(W):
                for have in (1, 2, 4):
                    shape = [have, SG]
                    top = [W[:, r, have - 1:have, :].to_broadcast([P] + shape) for r in range(2)]
                    cmul(W[:, 0, have:2 * have, :], W[:, 1, have:2 * have, :], W[:, 0, 0:have, :], W[:, 1, 0:have, :], top[0], top[1], temps(shape))

            need("mod0_pe")
            powers(POW)
            do(ve.memset(EXPO[:, 0, :, :], 1.0))
            do(ve.memset(EXPO[:, 1, :, :], 0.0))
            settle()
            copy(EXPO[0:SS, :, 1:L, :], POW[0:SS, :, 0:L - 1, :])
            copy(EXPO[SS:P, :, 0:L - 1, :], POW[SS:P, :, L - 2::-1, :])
            need("braw_ld", 64)
            bsh = [P, SG, SH]
            g16 = lambda v: v.unsqueeze(2).to_broadcast(bsh)
            cmul(BP[:, 0, :, :], BP[:, 1, :, :], g16(br_), g16(bi_), BRAW[:, 0, :, :], BRAW[:, 1, :, :], temps([SG, SH]))
            do(ve.memset(BB, 0.0))
            settle()
            for z in range(2):
                copy(BB[z * SS:(z + 1) * SS, :, :, z, :], BP[z * SS:(z + 1) * SS, :, :, :])
            settle()
            cmul(BP[:, 0, :, :], BP[:, 1, :, :], g16(POW[:, 0, 0, :]), g16(POW[:, 1, 0, :]), BP[:, 0, :, :], BP[:, 1, :, :], temps([SG, SH]))
            b4 = [P, SG, L, SH]
            er, ei = (EXPO[:, r, ::-1, :].rearrange("p j g -> p g j").unsqueeze(3).to_broadcast(b4) for r in range(2))
            pr, pi = (BP[:, r, :, :].unsqueeze(2).to_broadcast(b4) for r in range(2))
            tt(TMP[0], er, pr, ALU.mult)
            tt(TMP[1], ei, pi, ALU.mult)
            tt(W1N[:, 1, :, :, :], er, pi, ALU.mult)
            settle()
            tt(W1N[:, 0, :, :, :], TMP[0], TMP[1], ALU.subtract)
            settle()
            tt(TMP[0], ei, pr, ALU.mult)
            settle()
            tt(W1N[:, 1, :, :, :], W1N[:, 1, :, :, :], TMP[0], ALU.add)
            er, ei = (EXPO[:, r, :, :].rearrange("p j g -> p g j").unsqueeze(3).to_broadcast(b4) for r in range(2))
            cr, ci = (CT[:, r, :, :].unsqueeze(2).to_broadcast(b4) for r in range(2))
            tt(TMP[1], er, cr, ALU.mult)
            settle()
            tt(TMP[0], ei, ci, ALU.mult)
            settle()
            tt(CMV[:, 0, :, :, :], TMP[1], TMP[0], ALU.subtract)
            settle()
            tt(TMP[0], er, ci, ALU.mult)
            tt(TMP[1], ei, cr, ALU.mult)
            settle()
            stt(CMV[:, 1, :, :, :], TMP[0], -1.0, TMP[1], ALU.mult, ALU.subtract)
            settle()
            copy(PA[:, :, 0, :], POW[:, :, L - 1, :])
            settle()
            powers(PA)
            cmul(PAR[:, 4, 0, :], PAI[:, 4, 1, :], PA[:, 0, 7, :], PA[:, 1, 7, :], PA[:, 0, 7, :], PA[:, 1, 7, :], temps([SG]))
            copy(PAR[:, 4, 1, :], PAR[:, 4, 0, :])
            ts(PAI[:, 4, 0, :], PAI[:, 4, 1, :], -1.0, None, ALU.mult)
            for lev in range(4):
                k = 2 ** lev - 1
                for r in range(2):
                    copy(PAR[:, lev, r, :], PA[:, 0, k, :])
                    ts(PAI[:, lev, r, :], PA[:, 1, k, :], -1.0 if r == 0 else 1.0, None, ALU.mult)
            tell("tabs_ok")

            need("bcx_ok", 6)
            z_ = BCX[:, 2:4, :]
            tt(z_, BCX[:, 2:4, :], BCX[:, 4:6, :], ALU.mult)
            settle()
            for m_ in range(2):
                tap = [VEC[:, V_TAPS + 2 * w + m_:V_TAPS + 2 * w + m_ + 1] for w in range(3)]
                o, zz = YCONV[:, m_, :], BCX[:, 2 + m_, :]
                ts(o, zz, tap[1], None, ALU.mult)
                settle()
                stt(o[:, 1:T], zz[:, 0:T - 1], tap[0], o[:, 1:T], ALU.mult, ALU.add)
                settle()
                stt(o[:, 0:T - 1], zz[:, 1:T], tap[2], o[:, 0:T - 1], ALU.mult, ALU.add)
                settle()
            tt(YCONV, YCONV, BCX[:, 0:2, :], ALU.mult)
            tell("yconv_ok")

            need("qk_ld", 80)
            need("kcx_ok", 2)
            need("qk_ok", 4)
            HH = NQ + NKV
            QF = QK[:, :, :, :].rearrange("p t h d -> p (t h) d")
            SQ = down_w[:, 4096:5376].rearrange("p (h d) -> p h d", d=HD)
            KF = KCX[:, :, :, :].rearrange("p t h d -> p (t h) d")
            tt(SQ, QF, QF, ALU.mult)
            settle()
            do(ve.tensor_reduce(QST[:, 24:44], SQ, AX.X, ALU.add))
            settle()
            tt(SQ[:, 0:4, :], KF, KF, ALU.mult)
            settle()
            do(ve.tensor_reduce(QST[:, 44:48], SQ[:, 0:4, :], AX.X, ALU.add))
            settle()
            ts(QST[:, 24:48], QST[:, 24:48], 1.0 / HD, EPS, ALU.mult, ALU.add)
            tell("qss")
            need("qrs")
            do(ve.reciprocal(QST[:, 48:72], QST[:, 0:24]))
            settle()
            tt(QF, QF, QST[:, 48:68].unsqueeze(2).to_broadcast([P, TT * HH, HD]), ALU.mult)
            tt(KF, KF, QST[:, 68:72].unsqueeze(2).to_broadcast([P, TT * NKV, HD]), ALU.mult)
            settle()
            for t_ in range(TT):
                tt(QK[:, t_, 0:NQ, :], QK[:, t_, 0:NQ, :], QKG[:, 0:1, :].to_broadcast([P, NQ, HD]), ALU.mult)
                tt(QK[:, t_, NQ:HH, :], QK[:, t_, NQ:HH, :], QKG[:, 1:2, :].to_broadcast([P, NKV, HD]), ALU.mult)
            tt(KF, KF, QKG[:, 1:2, :].to_broadcast([P, TT * NKV, HD]), ALU.mult)
            settle()
            half = HD // 2
            shape = [P, TT, HH, half]
            co, si = COS.unsqueeze(2).to_broadcast(shape), SIN.unsqueeze(2).to_broadcast(shape)
            QPH = QP[:, :, :, :].rearrange("p t i (g d) -> p t (i g) d", g=2)
            rt1 = PR[:, 0, :, :].rearrange("p h k -> p (h k)")[:, 0:TT * HH * half].rearrange("p (t h d) -> p t h d", t=TT, h=HH)
            rt2 = PR[:, 1, :, :].rearrange("p h k -> p (h k)")[:, 0:TT * HH * half].rearrange("p (t h d) -> p t h d", t=TT, h=HH)
            x1, x2 = QK[:, :, :, 0:half], QK[:, :, :, half:HD]
            need("mz_pe")
            tt(QPH[:, :, :, 0:half], x1, co, ALU.mult)
            tt(rt1, x2, si, ALU.mult)
            tt(QPH[:, :, :, half:HD], x1, si, ALU.mult)
            tt(rt2, x2, co, ALU.mult)
            settle()
            tt(QPH[:, :, :, 0:half], QPH[:, :, :, 0:half], rt1, ALU.subtract)
            tt(QPH[:, :, :, half:HD], QPH[:, :, :, half:HD], rt2, ALU.add)
            tell("qp_ok")
            need("u2_pe")
            copy(U2[:, :, :].rearrange("p (b g) c -> p b (g c)", b=2), PS[:, 4:6, :])
            tell("u2_ok")
            need("bias_ld", 128)
            need("rb_free", 1)
            tt(MODR[1], PS[:, 6, :], MODR[1], ALU.add)
            tell("mod_row")
            need("tz_ld", 16 * 15)
            do(ve.memset(KT, 0.0))
            settle()
            need("qt_pe")
            for g in range(NKV):
                copy(KT[g * HD:(g + 1) * HD, g, :], PS[g * HD:(g + 1) * HD, 6, :])
            tell("qt_ok")
            need("inc_pe")
            copy(ZS[0:SS, :, :, :].rearrange("p r (b g) c -> p (r b) (g c)", b=2), PS[0:SS, 0:4, :])
            tell("zs_ok")
            def states_by_place():
                need("scan_ok")
                carry = [31, 3, 7, 11]
                for z in range(2):
                    h = slice(z * SS, (z + 1) * SS)
                    for s_ in range(4):
                        at = s_ * 8
                        if z == 0:
                            first, rest = ZR[h, :, :, at:at + 1], ZR[h, :, :, at + 1:at + 8]
                        else:
                            first = ZR[h, :, :, CCH - 1 - at:CCH - at]
                            lo = CCH - 8 - at
                            rest = ZR[h, :, :, lo:lo + 7][:, :, :, ::-1]
                        copy(first, ZS[h, :, :, carry[s_]:carry[s_] + 1])
                        copy(rest, ZS[h, :, :, CCH + at:CCH + at + 7])
                tell("zr_ok")

            need("mask_ld", 16)
            for k in range(2 * NP):
                if k == 4:
                    states_by_place()
                t_, i, b = k // NP, k % NP, k % 2
                need("s_pe", k + 1)
                if k >= 2:
                    need("pt_pe", k - 1)
                stt(PR[:, b, :, :], PS[:, 0:2, :], HD ** -0.5, MASK[:, t_:t_ + 1, :].to_broadcast([P, 2, BANK]), ALU.mult, ALU.add)
                tell("s_ok")
                do(ve.tensor_reduce(AC[:, b, 0:2], PR[:, b, :, :], AX.X, ALU.max))
                settle()
                tt(AC[:, b, 0:2], AC[:, b, 0:2], SINKS[:, i::NP], ALU.max)
                settle()
                ts(AC[:, b, 2:4], AC[:, b, 0:2], -1.0, None, ALU.mult)
                tt(AC[:, b, 8:10], SINKS[:, i::NP], AC[:, b, 0:2], ALU.subtract)
                tell("smax")
                need("sexp", k + 1)
                tt(AC[:, b, 10:12], AC[:, b, 6:8], AC[:, b, 4:6], ALU.add)
                settle()
                do(ve.reciprocal(AC[:, b, 10:12], AC[:, b, 10:12]))
                settle()
                for g in range(2):
                    ts(PR[:, b, g, :], PR[:, b, g, :], AC[:, b, 10 + g:11 + g], None, ALU.mult)
                tell("p_ok")
            need("wm2_pe", KC)
            tt(MODR[2], PS[:, 6, :], MODR[2], ALU.add)
            tell("mod_row")
            need("yt_pe")
            for m_ in range(2):
                stt(YS[:, m_, :].rearrange("p (c j) -> p c j", j=L), UT[:, m_, T:2 * T].rearrange("p (c j) -> p c j", j=L), VEC[:, V_D + m_:V_D + m_ + 1],
                    PS[:, 7, m_ * T:(m_ + 1) * T].rearrange("p (j c) -> p c j", j=L), ALU.mult, ALU.add)
            settle()
            yf = YS[:, :, :].rearrange("p m t -> p (m t)")
            tt(YT1, yf, yf, ALU.mult)
            settle()
            ts(YT1, YT1, GELU_C, 1.0, ALU.mult, ALU.add)
            settle()
            tt(YT1, YT1, yf, ALU.mult)
            tell("gelu_in")
            need("gelu_sg")
            tt(yf, yf, YG, ALU.mult)
            tell("z_ok")
            need("glu_ok")
            tt(YA[:, :, :].rearrange("p m t -> p (m t)"), yf, YG, ALU.mult)
            tell("yssm_ok")
            need("n2_ld", 16)
            need("row_ok", 1)
            stt(A2ROW, A2ROW, 1.0, N2ROW, ALU.add, ALU.mult)
            tell("a2_ok")
            for m_ in range(KC):
                b = 4 + 2 * (m_ % 2)
                need("br_pe", m_ + 1)
                g_ = SG_[:, m_, :, :]
                tt(g_[:, 0:2, :], g_[:, 0:2, :], PS[:, b, :].rearrange("p (s t) -> p s t", s=2), ALU.mult)
                tt(g_[:, 2, :], g_[:, 2, :], PS[:, b + 1, 0:T], ALU.mult)
                settle()
                tt(g_[:, 1, :], g_[:, 1, :], g_[:, 2, :], ALU.add)
                settle()
                tt(MERG[:, m_, :], g_[:, 0, :], g_[:, 1, :], ALU.add)
                tell("merg_ok")
            need("row_ok", 4)
            for t_ in range(TT):
                need("wo_pe", t_ + 1)
                mix = H2[:, t_, :]
                tt(mix.rearrange("p (b n) -> p b n", b=2), PS[:, 2 * t_:2 * t_ + 2, :], G1ROW[:, :].rearrange("p (b n) -> p b n", b=2), ALU.mult)
                settle()
                tt(X[:, t_, :], X[:, t_, :], mix, ALU.add)
                tell("x1_ok")
                tt(H2[:, t_, :], X[:, t_, :], A2ROW, ALU.mult)
                need("ss2", t_ + 1)
                ts(STAT[:, 4 + t_:5 + t_], STAT[:, t_:t_ + 1], 1.0 / D, EPS, ALU.mult, ALU.add)
                tell("ss2_ok")
                need("sd2", t_ + 1)
                do(ve.reciprocal(STAT[:, 12 + t_:13 + t_], STAT[:, 8 + t_:9 + t_]))
                settle()
                stt(H2[:, t_, :], H2[:, t_, :], STAT[:, 12 + t_:13 + t_], S2ROW, ALU.mult, ALU.add)
                tell("h2_ok")
            need("h2t_ok", TT)
            do(ve.memset(PS[:, 0:4, :], 0.0))
            need("rt_pe")
            for t_ in range(TT):
                copy(LG[:, t_, :], PS[:, 4, t_ * 64:t_ * 64 + NE])
            settle()
            for t_ in range(TT):
                do(ve.max(V8[:, t_, :], LG[:, t_, :]))
            settle()
            for t_ in range(TT):
                do(ve.max_index(I8[:, t_, :], V8[:, t_, :], LG[:, t_, :]))
                ts(NV0[:, t_:t_ + 1], V8[:, t_, 0:1], -1.0, None, ALU.mult)
            tell("ex_in")
            copy(I8F[:, :, :], I8[:, :, :])
            settle()
            for t_ in range(TT):
                shape4 = [P, NE, 4]
                tt(HIT[:, t_, :, :], IOTA[:, 0:NE].unsqueeze(2).to_broadcast(shape4), I8F[:, t_, 0:4].unsqueeze(1).to_broadcast(shape4), ALU.is_equal)
            settle()
            do(ve.tensor_reduce(MK, HIT, AX.X, ALU.add))
            tell("mk_ok")
            need("ex_out")
            do(ve.reciprocal(ERCP[:, 0:2], ESUM[:, 0:2]))
            settle()
            tt(G4[:, :, 0:4], E4[:, :, 0:4], ERCP[:, 0:2].unsqueeze(2).to_broadcast([P, TT, 4]), ALU.mult)
            settle()
            for t_ in range(TT):
                shape4 = [P, NE, 4]
                tt(HIT[:, t_, :, :], HIT[:, t_, :, :], G4[:, t_, 0:4].unsqueeze(1).to_broadcast(shape4), ALU.mult)
            settle()
            do(ve.tensor_reduce(GM, HIT, AX.X, ALU.add))
            tell("gm_ok")
            need("pos_pe")
            copy(CNT[0:NE, :], PS[0:NE, 7, 128:129])
            settle()
            ts(TE[0:NE, 0, 0:3], IOTA[0:NE, 1:4], float(NB), CNT[0:NE, :], ALU.mult, ALU.is_lt)
            settle()
            do(ve.tensor_reduce(NBK[0:NE, :], TE[0:NE, 0, 0:3], AX.X, ALU.add))
            settle()
            ts(NBK[0:NE, :], NBK[0:NE, :], 1.0, None, ALU.add)
            tell("tab")
            for t_ in range(TT):
                stt(PM[:, t_, :], PS[:, 7, t_ * 64:t_ * 64 + NE], 1.0, MK[:, t_, :], ALU.add, ALU.mult)
            settle()
            ts(PM, PM, -1.0, None, ALU.add)
            need("qs_pe")
            copy(qs_t[:, :], PS[0:1, 6, 0:NE + 1])
            tell("qs_ok")
            need("gt_pe")
            need("yc", 1)
            for h in range(2):
                copy(SELGT[h * NB:h * NB + NE, h, :], PS[h * NB:h * NB + NE, 5, 0:T])
            tell("gt_ok")
            ve.sem_inc(S["shift"], 1)
            ve.sem_inc(S["selgt"], 1)
            with ve.Fori(0, NE // 2) as pair:
                for par in range(2):
                    e = pair * 2 + par
                    first = ve.value_load(qs_t[0:1, bass.ds(e, 1)], min_val=0, max_val=4 * NE)
                    end = ve.value_load(qs_t[0:1, bass.ds(e + 1, 1)], min_val=1, max_val=4 * NE)
                    with ve.Fori(first, end) as q:
                        ve.wait_ge(S["shift"], q + 1)
                        ve.wait_ge(S["selgt"], q + 1)
                        for t in range(TT):
                            ve.tensor_scalar(SEL[:, t, :], IOTA[:, 0:NB], PM[:, t, bass.ds(e, 1)], None, ALU.is_equal)
                            last = ve.tensor_scalar(SELG[:, t, :], IOTA[:, 0:NB], PM[:, t, bass.ds(e, 1)], GM[:, t, bass.ds(e, 1)], ALU.is_equal, ALU.mult)
                        last.then_inc(S["sel"], 1)
                        ve.wait_ge(S["sel"], q + 1)
                        ve.tensor_scalar(PM[:, :, bass.ds(e, 1)], PM[:, :, bass.ds(e, 1)], float(-NB), None, ALU.add).then_inc(S["shift"], 1)
                        ve.wait_ge(S["xt"], q + 1)
                        ve.tensor_copy(XG[:, :, :].rearrange("p (b c) n -> p b (c n)", b=2), PS[:, 4:6, T:2 * T]).then_inc(S["xg"], 1)
                        for j in range(2):
                            s = slice(T * j, T * (j + 1))
                            ve.wait_ge(S["gup"], 2 * q + j + 1)
                            ve.tensor_scalar(GL[:, s], PS[:, 4 + j, 0::2], LIMIT, None, ALU.min).then_inc(S["glu"], 1)
                            ve.tensor_scalar(UP[:, s], PS[:, 4 + j, 1::2], LIMIT, -LIMIT, ALU.min, ALU.max).then_inc(S["actm"], 1)
                            ve.wait_ge(S["glu"], 2 * q + j + 1)
                            ve.wait_ge(S["actm"], 4 * q + 2 * j + 1)
                            ve.scalar_tensor_tensor(out=UP[:, s], in0=UP[:, s], scalar=1.0, in1=GL[:, s], op0=ALU.add, op1=ALU.mult).then_inc(S["actm"], 1)
                            ve.wait_ge(S["actm"], 4 * q + 2 * j + 2)
                            ve.wait_ge(S["sg"], 2 * q + j + 1)
                            ve.tensor_tensor(ACTA[:, s], UP[:, s], ACTA[:, s], ALU.mult).then_inc(S["act"], 1)
            ve.sem_inc(S["sel"], 1)
            blocks = ve.value_load(qs_t[0:1, NE:NE + 1], min_val=1, max_val=4 * NE)
            for t_ in range(TT):
                ve.wait_ge(S["scat"], blocks * 2 + (t_ + 1))
                tt(H2[:, t_, :].rearrange("p (b n) -> p b n", b=2), PS[:, 2 * t_:2 * t_ + 2, :], G2ROW[:, :].rearrange("p (b n) -> p b n", b=2), ALU.mult)
                settle()
                ve.tensor_tensor(X[:, t_, :], X[:, t_, :], H2[:, t_, :], ALU.add).then_inc(S["fin"], 1)


def tables():
    tok = np.arange(T)
    n_pairs = HD // 4
    inv = (10000.0 ** (-np.arange(n_pairs, dtype=np.float32) / n_pairs)).astype(np.float32)
    ang = np.concatenate([(tok // GRID_W).astype(np.float32)[:, None] * inv, (tok % GRID_W).astype(np.float32)[:, None] * inv], axis=-1)
    far = np.abs(tok[:, None] - tok[None, :]) > 128
    return {
        "ident": np.eye(P, dtype=np.float32),
        "before": np.triu(np.ones((P, P), np.float32), 1),
        "iota": np.tile(np.arange(NB, dtype=np.float32), (P, 1)),
        "cosine": np.cos(ang).astype(np.float32),
        "sine": np.sin(ang).astype(np.float32),
        "window": np.concatenate([np.zeros((T, T)), np.where(far, NEG, 0.0)], axis=1).astype(np.float32),
    }


NAMES = """x c ctx c_ctx w_mod b_mod norm1_g norm2_g w_in ssm_lam_re ssm_lam_im ssm_log_dt ssm_b_re ssm_b_im
    ssm_c_re ssm_c_im ssm_d w_glu w_ssm_out conv_w w_conv_out q_norm_g k_norm_g attn_sinks w_attn_out w_o
    w_router b_router w_gate_up b_gate_up w_down b_down""".split()


def kernel(**inputs):
    from concourse import bacc
    from concourse.bass_utils import run_bass_kernel_spmd

    nc = bacc.Bacc("TRN2", target_bir_lowering=False, num_devices=1)
    arrays = {n: np.ascontiguousarray(inputs[n]) for n in NAMES}
    arrays.update(tables())
    args = {n: nc.dram_tensor(f"in_{n}", a.shape, mybir.dt.from_np(a.dtype), kind="ExternalInput").ap() for n, a in arrays.items()}
    out = nc.dram_tensor("out", (1, T, D), F32, kind="ExternalOutput").ap()
    build(nc, out=out, **args)
    r = run_bass_kernel_spmd(nc, [{f"in_{n}": a for n, a in arrays.items()}], core_ids=[0])
    return r.results[0]["out"]
```
